# Optimizing a Trainium2 kernel written in Bass

```python
import jax, jax.numpy as jnp
from jax import lax
import numpy as np

D_MODEL = 1024
BATCH = 1
SEQ = 1024
DEPTH = 2
DEC_BATCH = 8
DEC_SEQ = 1
PAST_LEN = 4096
PAGE_SIZE = 128

HEAD_DIM = 64
A_WIDTH = D_MODEL // 2
CONV_W = 3
B_HEADS = (D_MODEL // 2) // HEAD_DIM
B_KV_HEADS = 2
SWA_WINDOW = 128
C_WIDTH = D_MODEL // 2
POOL_WINDOWS = (2, 4, 8, 16)
POOL_GROUPS = len(POOL_WINDOWS)
POOL_GC = C_WIDTH // POOL_GROUPS
POOL_PAD = max(POOL_WINDOWS) - 1
D_HEADS = (D_MODEL // 2) // HEAD_DIM
DIL_PATTERNS = ((128, 1), (512, 4), (2048, 16))
DIL_MAX_WINDOW = max(w for w, _ in DIL_PATTERNS)
MEM_LEN = 256
CA_HEADS = 4
CA_HEAD_DIM = D_MODEL // CA_HEADS
FFN_HIDDEN = -(-8 * D_MODEL // (3 * 256)) * 256
N_EVEN = (DEPTH + 1) // 2
N_ODD = DEPTH // 2
EVEN_IN = 3 * A_WIDTH + (B_HEADS + 2 * B_KV_HEADS) * HEAD_DIM
EVEN_SPLITS = (A_WIDTH, 2 * A_WIDTH, 3 * A_WIDTH, 3 * A_WIDTH + B_HEADS * HEAD_DIM,
               3 * A_WIDTH + (B_HEADS + B_KV_HEADS) * HEAD_DIM)
EVEN_MIX = A_WIDTH + B_HEADS * HEAD_DIM
ODD_IN = C_WIDTH + 3 * D_HEADS * HEAD_DIM
ODD_SPLITS = (C_WIDTH, C_WIDTH + D_HEADS * HEAD_DIM, C_WIDTH + 2 * D_HEADS * HEAD_DIM)
ODD_MIX = C_WIDTH + D_HEADS * HEAD_DIM
RMS_EPS = 1e-6
NEG_INF = -1e30

kernel_name = "hybrid_conv_swa_pool_dilated_decoder_step"

def rms_norm(x, g):
    xf = x.astype(jnp.float32)
    y = xf * lax.rsqrt(jnp.mean(xf * xf, axis=-1, keepdims=True) + RMS_EPS)
    return (y * g.astype(jnp.float32)).astype(x.dtype)

def attend(q, k, v, mask):
    *lead, tq, h, dh = q.shape
    hk = k.shape[-2]
    qg = q.reshape(*lead, tq, hk, h // hk, dh)
    s = jnp.einsum("...qhgd,...khd->...hgqk", qg, k, preferred_element_type=jnp.float32) * (dh ** -0.5)
    s = jnp.where(mask[..., None, None, :, :], s, NEG_INF)
    lse = jax.nn.logsumexp(s, axis=-1)
    p = jnp.exp(s - lse[..., None]).astype(v.dtype)
    o = jnp.einsum("...hgqk,...khd->...qhgd", p, v).reshape(*lead, tq, h, dh)
    lse = jnp.swapaxes(lse.reshape(*lead, h, tq), -1, -2)
    return o, lse

def band_attn(q, k, v, window):
    bn, L, h, dh = q.shape
    blk = window
    nb = -(-L // blk)
    pad = nb * blk - L
    qb = jnp.pad(q, ((0, 0), (0, pad), (0, 0), (0, 0))).reshape(bn, nb, blk, h, dh)

    def key_blocks(a):
        a = jnp.pad(a, ((0, 0), (blk, pad), (0, 0), (0, 0))).reshape(bn, nb + 1, blk, a.shape[2], dh)
        return jnp.concatenate([a[:, :-1], a[:, 1:]], axis=2)

    kb, vb = key_blocks(k), key_blocks(v)
    ki = jnp.arange(2 * blk)
    delta = (jnp.arange(blk)[:, None] + blk) - ki[None, :]
    kabs = (jnp.arange(nb)[:, None, None] - 1) * blk + ki[None, None, :]
    mask = (delta >= 0)[None] & (delta <= window)[None] & (kabs >= 0)
    o, lse = attend(qb, kb, vb, mask)
    return o.reshape(bn, nb * blk, h, dh)[:, :L], lse.reshape(bn, nb * blk, h)[:, :L]

def apply_sinks(o, lse, sinks):
    gate = jax.nn.sigmoid(lse - sinks.astype(jnp.float32))
    return (o * gate[..., None]).astype(o.dtype)

def combine_branches(outs, lses):
    wts = jax.nn.softmax(jnp.stack(lses), axis=0)
    y = sum(wts[i][..., None] * outs[i] for i in range(len(outs)))
    return y.astype(outs[0].dtype)

def dilated_prompt(q, k, v):
    bn, L, h, dh = q.shape
    outs, lses = [], []
    for w, d in DIL_PATTERNS:
        def sub(a):
            return a.reshape(bn, L // d, d, a.shape[2], dh).transpose(0, 2, 1, 3, 4).reshape(bn * d, L // d, a.shape[2], dh)
        o, lse = band_attn(sub(q), sub(k), sub(v), w // d)
        outs.append(o.reshape(bn, d, L // d, h, dh).transpose(0, 2, 1, 3, 4).reshape(bn, L, h, dh))
        lses.append(lse.reshape(bn, d, L // d, h).transpose(0, 2, 1, 3).reshape(bn, L, h))
    return combine_branches(outs, lses)

def dilated_sample(q, k_buf, v_buf, k, v):
    bn, t, h, dh = q.shape
    nbuf = k_buf.shape[1]
    kc = jnp.concatenate([k_buf, k], axis=1)
    vc = jnp.concatenate([v_buf, v], axis=1)
    qpos = PAST_LEN + jnp.arange(t)
    outs, lses = [], []
    for w, d in DIL_PATTERNS:
        kpos = qpos[:, None] - d * jnp.arange(w // d + 1)[None, :]
        idx = jnp.clip(kpos - (PAST_LEN - nbuf), 0, nbuf + t - 1)
        o, lse = attend(q[:, :, None], kc[:, idx], vc[:, idx], (kpos >= 0)[:, None, :])
        outs.append(o[:, :, 0])
        lses.append(lse[:, :, 0])
    return combine_branches(outs, lses)

def short_conv(upad, w):
    L = upad.shape[1] - (CONV_W - 1)
    return sum(w[i] * upad[:, i:i + L] for i in range(CONV_W))

def pool_mix(upad, u, pos, pool_w, pool_scale):
    bn, L, c = u.shape
    cs = jnp.pad(jnp.cumsum(upad.astype(jnp.float32), axis=1), ((0, 0), (1, 0), (0, 0)))
    top = cs[:, POOL_PAD + 1:]
    means = []
    for g, w in enumerate(POOL_WINDOWS):
        sl = slice(g * POOL_GC, (g + 1) * POOL_GC)
        win_sum = top[:, :, sl] - cs[:, POOL_PAD + 1 - w:POOL_PAD + 1 - w + L, sl]
        cnt = jnp.minimum(pos + 1, w).astype(jnp.float32)[:, None]
        means.append(win_sum / cnt)
    dlt = (jnp.concatenate(means, axis=-1) - u.astype(jnp.float32)).astype(u.dtype)
    y = jnp.einsum("blgc,gcd->blgd", dlt.reshape(bn, L, POOL_GROUPS, POOL_GC), pool_w)
    return y.reshape(bn, L, c) * pool_scale

def even_mixer_prompt(h, w_in, conv_w, sinks, w_out):
    bn, L, _ = h.shape
    bg, cg, xa, q, k, v = jnp.split(h @ w_in, EVEN_SPLITS, axis=-1)
    u = cg * xa
    upad = jnp.concatenate([jnp.zeros((bn, CONV_W - 1, A_WIDTH), u.dtype), u], axis=1)
    ya = bg * short_conv(upad, conv_w)
    q = q.reshape(bn, L, B_HEADS, HEAD_DIM)
    k = k.reshape(bn, L, B_KV_HEADS, HEAD_DIM)
    v = v.reshape(bn, L, B_KV_HEADS, HEAD_DIM)
    o, lse = band_attn(q, k, v, SWA_WINDOW)
    yb = apply_sinks(o, lse, sinks)
    out = jnp.concatenate([ya, yb.reshape(bn, L, -1)], axis=-1) @ w_out
    keep = min(SWA_WINDOW, L)
    return out, u[:, L - (CONV_W - 1):], k[:, L - keep:], v[:, L - keep:]

def even_mixer_sample(h, conv_buf, k_buf, v_buf, w_in, conv_w, sinks, w_out):
    bn, t, _ = h.shape
    bg, cg, xa, q, k, v = jnp.split(h @ w_in, EVEN_SPLITS, axis=-1)
    upad = jnp.concatenate([conv_buf, cg * xa], axis=1)
    ya = bg * short_conv(upad, conv_w)
    q = q.reshape(bn, t, B_HEADS, HEAD_DIM)
    k = k.reshape(bn, t, B_KV_HEADS, HEAD_DIM)
    v = v.reshape(bn, t, B_KV_HEADS, HEAD_DIM)
    nbuf = k_buf.shape[1]
    kc = jnp.concatenate([k_buf, k], axis=1)
    vc = jnp.concatenate([v_buf, v], axis=1)
    qpos = PAST_LEN + jnp.arange(t)
    kpos = PAST_LEN - nbuf + jnp.arange(nbuf + t)
    delta = qpos[:, None] - kpos[None, :]
    o, lse = attend(q, kc, vc, (delta >= 0) & (delta <= SWA_WINDOW))
    yb = apply_sinks(o, lse, sinks)
    out = jnp.concatenate([ya, yb.reshape(bn, t, -1)], axis=-1) @ w_out
    return out, upad[:, -(CONV_W - 1):], k, v

def odd_mixer_prompt(h, w_in, pool_w, pool_scale, w_out):
    bn, L, _ = h.shape
    uc, q, k, v = jnp.split(h @ w_in, ODD_SPLITS, axis=-1)
    upad = jnp.concatenate([jnp.zeros((bn, POOL_PAD, C_WIDTH), uc.dtype), uc], axis=1)
    yc = pool_mix(upad, uc, jnp.arange(L), pool_w, pool_scale)
    q = q.reshape(bn, L, D_HEADS, HEAD_DIM)
    k = k.reshape(bn, L, D_HEADS, HEAD_DIM)
    v = v.reshape(bn, L, D_HEADS, HEAD_DIM)
    yd = dilated_prompt(q, k, v)
    out = jnp.concatenate([yc, yd.reshape(bn, L, -1)], axis=-1) @ w_out
    keep = min(DIL_MAX_WINDOW, L)
    return out, uc[:, L - POOL_PAD:], k[:, L - keep:], v[:, L - keep:]

def odd_mixer_sample(h, pool_buf, k_buf, v_buf, w_in, pool_w, pool_scale, w_out):
    bn, t, _ = h.shape
    uc, q, k, v = jnp.split(h @ w_in, ODD_SPLITS, axis=-1)
    upad = jnp.concatenate([pool_buf, uc], axis=1)
    yc = pool_mix(upad, uc, PAST_LEN + jnp.arange(t), pool_w, pool_scale)
    q = q.reshape(bn, t, D_HEADS, HEAD_DIM)
    k = k.reshape(bn, t, D_HEADS, HEAD_DIM)
    v = v.reshape(bn, t, D_HEADS, HEAD_DIM)
    yd = dilated_sample(q, k_buf, v_buf, k, v)
    out = jnp.concatenate([yc, yd.reshape(bn, t, -1)], axis=-1) @ w_out
    return out, upad[:, -POOL_PAD:], k, v

def memory_kv(mem, g, w_kv):
    bn, m, _ = mem.shape
    mk, mv = jnp.split(rms_norm(mem, g) @ w_kv, 2, axis=-1)
    return mk.reshape(bn, m, CA_HEADS, CA_HEAD_DIM), mv.reshape(bn, m, CA_HEADS, CA_HEAD_DIM)

def cross_attn(h, mk, mv, w_q, w_o):
    bn, L, _ = h.shape
    q = (h @ w_q).reshape(bn, L, CA_HEADS, CA_HEAD_DIM)
    o, _ = attend(q, mk, mv, jnp.ones((L, mk.shape[1]), dtype=bool))
    return o.reshape(bn, L, -1) @ w_o

def swiglu(h, w_in, w_out):
    g, u = jnp.split(h @ w_in, 2, axis=-1)
    return (jax.nn.silu(g) * u) @ w_out

def setup_inputs(seed: int = 0) -> dict:
    key = jax.random.key(seed)
    ks = iter(jax.random.split(key, 40))

    def nrm(shape, scale=1.0):
        return scale * jax.random.normal(next(ks), shape, jnp.float32)

    swa_keep = min(SWA_WINDOW, PAST_LEN)
    dil_keep = min(DIL_MAX_WINDOW, PAST_LEN)
    return {
        "x_prompt": nrm((BATCH, SEQ, D_MODEL)),
        "x_sample": nrm((DEC_BATCH, DEC_SEQ, D_MODEL)),
        "mem_prompt": nrm((BATCH, MEM_LEN, D_MODEL)),
        "cache_conv": nrm((N_EVEN, DEC_BATCH, CONV_W - 1, A_WIDTH)),
        "cache_swa_k": nrm((N_EVEN, DEC_BATCH, swa_keep, B_KV_HEADS, HEAD_DIM)),
        "cache_swa_v": nrm((N_EVEN, DEC_BATCH, swa_keep, B_KV_HEADS, HEAD_DIM)),
        "state_pool": nrm((N_ODD, DEC_BATCH, POOL_PAD, C_WIDTH)),
        "cache_dil_k": nrm((N_ODD, DEC_BATCH, dil_keep, D_HEADS, HEAD_DIM)),
        "cache_dil_v": nrm((N_ODD, DEC_BATCH, dil_keep, D_HEADS, HEAD_DIM)),
        "cache_mem_k": nrm((DEPTH, DEC_BATCH, MEM_LEN, CA_HEADS, CA_HEAD_DIM)),
        "cache_mem_v": nrm((DEPTH, DEC_BATCH, MEM_LEN, CA_HEADS, CA_HEAD_DIM)),
        "norm_mix": 1.0 + nrm((DEPTH, D_MODEL), 0.05),
        "norm_ca": 1.0 + nrm((DEPTH, D_MODEL), 0.05),
        "norm_mem": 1.0 + nrm((DEPTH, D_MODEL), 0.05),
        "norm_ffn": 1.0 + nrm((DEPTH, D_MODEL), 0.05),
        "norm_final": 1.0 + nrm((D_MODEL,), 0.05),
        "w_in_even": nrm((N_EVEN, D_MODEL, EVEN_IN), D_MODEL ** -0.5),
        "conv_w": nrm((N_EVEN, CONV_W, A_WIDTH), CONV_W ** -0.5),
        "sinks": nrm((N_EVEN, B_HEADS), 0.5),
        "w_out_even": nrm((N_EVEN, EVEN_MIX, D_MODEL), EVEN_MIX ** -0.5),
        "w_in_odd": nrm((N_ODD, D_MODEL, ODD_IN), D_MODEL ** -0.5),
        "pool_w": nrm((N_ODD, POOL_GROUPS, POOL_GC, POOL_GC), POOL_GC ** -0.5),
        "pool_scale": 1.0 + nrm((N_ODD, C_WIDTH), 0.1),
        "w_out_odd": nrm((N_ODD, ODD_MIX, D_MODEL), ODD_MIX ** -0.5),
        "w_ca_q": nrm((DEPTH, D_MODEL, CA_HEADS * CA_HEAD_DIM), D_MODEL ** -0.5),
        "w_ca_kv": nrm((DEPTH, D_MODEL, 2 * CA_HEADS * CA_HEAD_DIM), D_MODEL ** -0.5),
        "w_ca_o": nrm((DEPTH, CA_HEADS * CA_HEAD_DIM, D_MODEL), (CA_HEADS * CA_HEAD_DIM) ** -0.5),
        "w_ffn_in": nrm((DEPTH, D_MODEL, 2 * FFN_HIDDEN), D_MODEL ** -0.5),
        "w_ffn_out": nrm((DEPTH, FFN_HIDDEN, D_MODEL), FFN_HIDDEN ** -0.5),
    }

def reference(x_prompt, x_sample, mem_prompt, cache_conv, cache_swa_k, cache_swa_v, state_pool,
              cache_dil_k, cache_dil_v, cache_mem_k, cache_mem_v, norm_mix, norm_ca, norm_mem,
              norm_ffn, norm_final, w_in_even, conv_w, sinks, w_out_even, w_in_odd, pool_w,
              pool_scale, w_out_odd, w_ca_q, w_ca_kv, w_ca_o, w_ffn_in, w_ffn_out):
    xp, xs = x_prompt, x_sample
    conv_p, swak_p, swav_p, pool_p, dilk_p, dilv_p, memk_p, memv_p = [], [], [], [], [], [], [], []
    conv_s, swak_s, swav_s, pool_s, dilk_s, dilv_s = [], [], [], [], [], []
    for l in range(DEPTH):
        hp = rms_norm(xp, norm_mix[l])
        hs = rms_norm(xs, norm_mix[l])
        if l % 2 == 0:
            e = l // 2
            op, cp, kp, vp = even_mixer_prompt(hp, w_in_even[e], conv_w[e], sinks[e], w_out_even[e])
            os_, cs_, ks_, vs_ = even_mixer_sample(hs, cache_conv[e], cache_swa_k[e], cache_swa_v[e],
                                                  w_in_even[e], conv_w[e], sinks[e], w_out_even[e])
            conv_p.append(cp); swak_p.append(kp); swav_p.append(vp)
            conv_s.append(cs_); swak_s.append(ks_); swav_s.append(vs_)
        else:
            o = l // 2
            op, cp, kp, vp = odd_mixer_prompt(hp, w_in_odd[o], pool_w[o], pool_scale[o], w_out_odd[o])
            os_, cs_, ks_, vs_ = odd_mixer_sample(hs, state_pool[o], cache_dil_k[o], cache_dil_v[o],
                                                 w_in_odd[o], pool_w[o], pool_scale[o], w_out_odd[o])
            pool_p.append(cp); dilk_p.append(kp); dilv_p.append(vp)
            pool_s.append(cs_); dilk_s.append(ks_); dilv_s.append(vs_)
        xp = xp + op
        xs = xs + os_
        mk, mv = memory_kv(mem_prompt, norm_mem[l], w_ca_kv[l])
        memk_p.append(mk); memv_p.append(mv)
        xp = xp + cross_attn(rms_norm(xp, norm_ca[l]), mk, mv, w_ca_q[l], w_ca_o[l])
        xs = xs + cross_attn(rms_norm(xs, norm_ca[l]), cache_mem_k[l], cache_mem_v[l], w_ca_q[l], w_ca_o[l])
        xp = xp + swiglu(rms_norm(xp, norm_ffn[l]), w_ffn_in[l], w_ffn_out[l])
        xs = xs + swiglu(rms_norm(xs, norm_ffn[l]), w_ffn_in[l], w_ffn_out[l])
    y_prompt = rms_norm(xp, norm_final)
    y_sample = rms_norm(xs, norm_final)
    return (y_prompt, y_sample,
            jnp.stack(conv_p), jnp.stack(swak_p), jnp.stack(swav_p),
            jnp.stack(pool_p), jnp.stack(dilk_p), jnp.stack(dilv_p),
            jnp.stack(memk_p), jnp.stack(memv_p),
            jnp.stack(conv_s), jnp.stack(swak_s), jnp.stack(swav_s),
            jnp.stack(pool_s), jnp.stack(dilk_s), jnp.stack(dilv_s))


_drawn_inputs = setup_inputs


def setup_inputs(seed=0):
    import zlib

    import numpy as np

    out = dict(_drawn_inputs(seed))
    spreads = {}
    factors = {'norm_ca': 8.0, 'sinks': 8.0}
    for name, (base, spread) in spreads.items():
        noise = np.random.default_rng([zlib.crc32(name.encode()), seed]).standard_normal(out[name].shape)
        drawn = base * np.exp(spread * noise) if base else spread * noise
        out[name] = __import__('jax').numpy.asarray(drawn.astype(out[name].dtype))
    for name, factor in factors.items():
        out[name] = (out[name] * factor).astype(out[name].dtype)
    return out
```

```python
from contextlib import ExitStack

import numpy as np

import concourse.bass as bass
from concourse import mybir

F32 = mybir.dt.float32
F32R = mybir.dt.float32r
ALU = mybir.AluOpType
ACT = mybir.ActivationFunctionType
AX_X = mybir.AxisListType.X

P = 128
D = 1024
SEQ = 1024
BATCH_S = 8
TOK = SEQ + BATCH_S
CH = D // P
TILE = TOK // 3
TILES = [(0, TILE), (TILE, 2 * TILE), (2 * TILE, TOK)]
MEM = 256
FFN = 2816
FFN_STEPS = FFN // 256
HEAD = 64
PAIRS = 4
CA_HEADS = 4
CONV_W = 3
POOL_WINDOWS = (2, 4, 8, 16)
POOL_PAD = 15
EPS = 1e-6
NEG = -1e30
DILATIONS = ((128, 1), (512, 4), (2048, 16))
QB = SEQ // P
GAINS = ["mix0", "mix1", "ca0", "ca1", "mem0", "mem1", "ffn0", "ffn1", "final"]
STASH = 22



def tile_plan(name):
    three = lambda who: [(b, who) for b in range(3)]
    if name == "kv0":
        return three("act") * 2
    if name == "att0":
        return three("act") + three("act") + three("dve") + three("dve")
    if name.startswith("out") or name.startswith("caout"):
        return three("dve") * 2
    if name.startswith("cross"):
        return [(b, "act") for b in (0, 1, 2, 0)] + [(1, "act"), (2, "act"), (0, "act")] + [(1, "act"), (2, "act"), (0, "act")]
    if name.startswith("ffn"):
        return (three("act") + three("dve")) * 2 + three("dve") * 8
    if name == "pool1":
        return three("act") * 4
    if name == "att1":
        return three("act") * 6
    return []


def job_events(n):
    return {e: n for e in ("scored", "peaked", "biased", "exped", "inverted", "normed", "turned", "turned_in",
                           "mixed", "mixed_out")}


def norm_events(tiles, split=True):
    e = {"squared": 2 * tiles, "summed": tiles, "rooted": tiles, "rsqrted": tiles, "scaled": 2 * tiles}
    if split:
        e |= {"hi_ready": 2 * tiles, "lo_ready": 2 * tiles}
    return e


def phases():
    out = []
    for l in range(2):
        out.append((f"norm_mix{l}", 1, 0, norm_events(3)))
        if l == 0:
            out.append(("kv0", 1, 2, {"v_turned": 1, "v_ready": 1}))
            out.append(("att0", PAIRS, 4, job_events(QB * 2 + 1) | {"q_spread": 1}))
        else:
            out.append(("pool1", 1, 4, {"delta_ready": 4, "pooled": 12, "pooled_out": 12}))
            out.append(("att1", PAIRS // 2, 6, {k: 2 * v for k, v in job_events(QB * 2 + 1).items()}
                        | {"q_spread": 2, "v_turned": 2, "v_ready": 2}))
        out.append((f"split{l}", 1, 0, {"hi_ready": 6, "lo_ready": 6}))
        out.append((f"out{l}", 4, 2, {}))
        out.append((f"norm_mem{l}", 1, 0, norm_events(1)))
        out.append((f"norm_ca{l}", 1, 0, norm_events(3)))
        out.append((f"cross{l}", CA_HEADS, 6, job_events(QB + 1) | {"q_spread": 1, "v_turned": 1, "v_ready": 1}))
        out.append((f"casplit{l}", 1, 0, {"hi_ready": 6, "lo_ready": 6}))
        out.append((f"caout{l}", 4, 2, {}))
        out.append((f"norm_ffn{l}", 1, 0, norm_events(3)))
        out.append((f"ffn{l}", FFN_STEPS, 6, {"hid_hi": 6, "hid_lo": 6}))
    out.append(("norm_final", 1, 0, norm_events(3, split=False)))
    for i, (name, turns, units, events) in enumerate(out):
        plan = tile_plan(name)
        events = dict(events)
        if plan:
            events |= {"tile_done": len(plan), "freed_act": sum(w == "act" for _, w in plan),
                       "freed_dve": sum(w == "dve" for _, w in plan)}
        if units:
            events |= {"unit_split": units, "unit_started": units}
        out[i] = (name, turns, units, events)
    return out


PHASES = phases()
CREDIT = {"unit_split": 2, "unit_started": 1, "freed_act": 4, "freed_dve": 4, "peaked": 1, "exped": 1,
          "turned": 1, "mixed_out": 1}
N_UNITS = sum(turns * units for _, turns, units, _ in PHASES)


def at(event, phase, turn=0, k=0):
    base = CREDIT.get(event, 0)
    for name, turns, _, events in PHASES:
        per = events.get(event, 0)
        if name == phase:
            return turn * per + (base + k)
        base += turns * per
    raise KeyError(phase)


def bank_wait(phase, turn, p):
    plan = tile_plan(phase)
    bank = plan[p][0]
    before = [j for j in range(p - 1, -1, -1) if plan[j][0] == bank]
    wrap = not before
    j = before[0] if before else max(i for i in range(len(plan)) if plan[i][0] == bank)
    who = plan[j][1]
    done = sum(w == who for _, w in plan[:j + 1])
    total = sum(w == who for _, w in plan)
    return f"freed_{who}", at(f"freed_{who}", phase, turn, done - (total if wrap else 0))


def freed_index(phase, p):
    plan = tile_plan(phase)
    return sum(w == plan[p][1] for _, w in plan[:p + 1])


def pipeline(n):
    yield "S", "sample"
    for s in range(n + 2):
        if s < n:
            yield "S", s
        if 0 <= s - 2 < n:
            yield "V", s - 2
        if 0 <= s - 1 < n:
            yield "T", s - 1
    yield "T", "sample"
    yield "V", "sample"


def order_s(job):
    return 0 if job == "sample" else job + 1


def order_t(job, n):
    return n if job == "sample" else job


def key_blocks(kind, job):
    qb = job % QB
    if kind == "swa":
        return max(0, qb - 1), min(2, qb + 1)
    if kind == "dil":
        return 0, qb + 1
    return 0, MEM // P


def slot_value(layer, crossing, turn, part=0):
    base, per = (0, 1) if layer == 0 else (8, 1) if crossing else (4, 2)
    return turn * (16 * per) + 16 * (base + part + 1)


def stored_before(layer, crossing, turn, part=0):
    base, per = (1, 1) if layer == 0 else (9, 1) if crossing else (5, 2)
    return turn * (16 * per) + 16 * (base + part)


KV_STORES = 16 * 13
ATT0_LOADS = 16 * 5
DVE_BASE = 1
CONV_STEPS = 5
DVE_PER_TURN = CONV_STEPS + 2 * QB + 1
CROSS_STEP = [DVE_BASE + PAIRS * DVE_PER_TURN + 1]
POOL_STEP = CROSS_STEP[0]
ATT1_STEP = POOL_STEP + 2 + sum(g + 5 for g in range(len(POOL_WINDOWS)))
CROSS_STEP.append(ATT1_STEP + 1)


def program(nc, dram):
    ctx = ExitStack()
    with ctx:
        cursor = [16512]

        def place(name, shape, dt=F32, offset=None):
            size = -(-int(np.prod(shape[1:])) * 4 // 32) * 32
            if offset is None:
                offset = cursor[0]
                cursor[0] += size
            assert offset + size <= 229344, (name, offset + size)
            return nc.alloc_sbuf_tensor_at(name, shape, dt, offset=offset)

        x = place("x", [P, CH, TOK])
        h_hi = place("h_hi", [P, CH, TOK], F32R)
        h_lo = place("h_lo", [P, CH, TOK], F32R)
        w_raw = place("w_raw", [P, 2, D])
        w_hi = place("w_hi", [P, 2, D], F32R)
        w_lo = place("w_lo", [P, 2, D], F32R)
        ident = place("ident", [P, P])
        ones = place("ones", [P, P])
        gains = place("gains", [P, len(GAINS), CH])
        eps = place("eps", [P, 1])
        peak = place("peak", [P, 2])
        bias = place("bias", [P, 2])
        den = place("den", [P, 2])
        sink_exp = place("sink_exp", [P, 2])
        inv = place("inv", [P, 2])
        token_mask = place("token_mask", [16, BATCH_S])
        sel = {kind: place(f"new_{kind}", [16, BATCH_S]) for kind in ("swa", "dil")}
        region = cursor[0]

        def over(*items):
            at_, out = region, []
            for name, shape, dt in items:
                out.append(place(name, shape, dt, offset=at_))
                at_ += -(-int(np.prod(shape[1:])) * 4 // 32) * 32
            return out

        sq, scaled, root, rsqrt, mem_in = over(
            ("sq", [P, 2, CH, TILE], F32), ("scaled", [P, 2, CH, TILE], F32), ("root", [P, 2, TILE], F32),
            ("rsqrt", [P, 2, TILE], F32), ("mem_in", [P, CH, MEM], F32))
        (mix0, q0, k0, v0, vnat0, vnew0, qd0, p0, pt0, ps0, smask0, mask0, ks0, vs0, cgate, conv_u, conv_t, stash,
         cur, sink8) = over(
            ("mix0", [P, CH, TOK], F32), ("q0", [P, TOK], F32), ("k0", [P, TOK], F32), ("v0", [P, TOK], F32),
            ("vnat0", [P, QB, P], F32), ("vnew0", [BATCH_S, P], F32), ("qd0", [P, BATCH_S, 16], F32),
            ("p0", [P, 2, 256], F32), ("pt0", [P, 256], F32), ("ps0", [16, 129], F32), ("smask0", [16, 129], F32),
            ("mask0", [P, 256], F32), ("ks0", [P, BATCH_S, 128], F32), ("vs0", [P, BATCH_S, 1, P], F32),
            ("cgate", [P, TOK], F32), ("conv_u", [P, 2 + TOK], F32), ("conv_t", [P, TOK], F32),
            ("stash", [P, PAIRS, STASH], F32), ("cur", [P, STASH], F32), ("sink8", [P, 3], F32))
        (mix1, q1, k1, v1, vnat1, vnew1, qd1, p1, pt1, ps1, smask1, mask1, kv_slot1) = over(
            ("mix1", [P, CH, TOK], F32), ("q1", [P, TOK], F32), ("k1", [P, TOK], F32), ("v1", [P, TOK], F32),
            ("vnat1", [P, QB, P], F32), ("vnew1", [BATCH_S, P], F32), ("qd1", [P, BATCH_S, 16], F32),
            ("p1", [P, 2, 1024], F32), ("pt1", [P, 1024], F32), ("ps1", [16, 385], F32), ("smask1", [16, 385], F32),
            ("mask1", [P, 1024], F32), ("kv_slot1", [P, BATCH_S * 384], F32))
        (_, pool_u, pool_a, pool_b, pool_d, pool_hist, pool_w, pool_rcp, pool_gain, pool_s) = over(
            ("mix1_", [P, CH, TOK], F32), ("pool_u", [P, POOL_PAD + TOK], F32), ("pool_a", [P, POOL_PAD + SEQ], F32),
            ("pool_b", [P, POOL_PAD + SEQ], F32), ("pool_d", [P, 2, TOK], F32),
            ("pool_hist", [P, 4, BATCH_S, POOL_PAD], F32), ("pool_w", [P, 4, P], F32), ("pool_rcp", [P, 4, 16], F32),
            ("pool_gain", [P, 4], F32), ("pool_s", [P, 2, BATCH_S], F32))
        (mixc, qc, kc, vc, vnatc, p_c, ptc, psc, qdc, kv_slotc, mem_hi, mem_lo) = over(
            ("mixc", [P, CH, TOK], F32), ("qc", [P, 2, TOK], F32), ("kc", [P, 2, MEM], F32), ("vc", [P, 2, MEM], F32),
            ("vnatc", [P, 2, MEM], F32), ("p_c", [P, 2, 256], F32), ("ptc", [P, 256], F32), ("psc", [8, 256], F32),
            ("qdc", [P, 2, BATCH_S, 8], F32), ("kv_slotc", [P, BATCH_S * 512], F32),
            ("mem_hi", [P, CH, MEM], F32R), ("mem_lo", [P, CH, MEM], F32R))
        hid_hi, hid_lo, gate, hid = over(
            ("hid_hi", [P, 2, TOK], F32R), ("hid_lo", [P, 2, TOK], F32R), ("gate", [P, TOK], F32), ("hid", [P, TOK], F32))

        lin = [ctx.enter_context(nc.psum_tensor(f"lin{i}", [P, 512], F32)) for i in range(3)]
        ps_s = ctx.enter_context(nc.psum_tensor("ps_scores", [P, 1024], F32))
        ps_t = ctx.enter_context(nc.psum_tensor("ps_turned", [P, 1024], F32))
        ps_o = ctx.enter_context(nc.psum_tensor("ps_mixed", [P, 512], F32))
        sum_banks = [ps_s[:, 0:512], ps_s[:, 512:1024], ps_t[:, 0:512]]

        names = sorted({e for _, _, _, ev in PHASES for e in ev})
        sem = {n: ctx.enter_context(nc.semaphore(n)) for n in names}
        gate_sem = {n: ctx.enter_context(nc.semaphore(f"passed_{n}")) for n in ("pe", "act", "dve", "pool")}
        dve_step = ctx.enter_context(nc.semaphore("dve_step"))
        landed = [ctx.enter_context(nc.semaphore(f"unit_landed{i}")) for i in range(2)]
        loads = {n: ctx.enter_context(nc.semaphore(f"load_{n}")) for n in
                 ("x", "consts", "att0", "pool1", "att1", "mem0", "mem1", "k_slot", "v_slot", "mask1")}
        consts_set = ctx.enter_context(nc.semaphore("consts_set"))
        pool_hi = ctx.enter_context(nc.semaphore("unit_hi"))
        stored = {n: ctx.enter_context(nc.semaphore(f"stored_{n}")) for n in ("k", "v", "u", "y0", "y1", "y2", "past")}
        block = ctx.enter_context(nc.Block())

        norms = []
        for l in range(2):
            norms += [(f"norm_mix{l}", f"mix{l}", x, TILES, h_hi, h_lo), (f"norm_mem{l}", f"mem{l}", mem_in, [(0, MEM)], mem_hi, mem_lo),
                      (f"norm_ca{l}", f"ca{l}", x, TILES, h_hi, h_lo), (f"norm_ffn{l}", f"ffn{l}", x, TILES, h_hi, h_lo)]
        norms.append(("norm_final", "final", x, TILES, None, None))
        norms = {n[0]: n[1:] for n in norms}

        @block.sync
        def _(sp):
            sp.dma_start(x[:], dram["x"]).then_inc(loads["x"], 16)
            sp.dma_start(gains[:], dram["gains"]).then_inc(loads["consts"], 16)
            sp.dma_start(ident[:], dram["ident"]).then_inc(loads["consts"], 16)
            sp.dma_start(token_mask[:], dram["token_mask"]).then_inc(loads["consts"], 16)
            sp.dma_start(dram["conv_past"], dram["cache_conv"][:, 1, :]).then_inc(stored["past"], 16)
            sp.dma_start(dram["pool_past"], dram["state_pool"][:, 1:, :]).then_inc(stored["past"], 16)
            with sp.Fori(0, N_UNITS // 2) as i:
                for s in range(2):
                    sp.wait_ge(sem["unit_split"], 2 * i + (s + 1))
                    sp.dma_start(w_raw[:, s, :], dram["w"][bass.ds(2 * i + s, 1)].rearrange("a p n -> p (a n)")
                                 ).then_inc(landed[s], 16)
            sp.wait_ge(stored["past"], 32)

        @block.gpsimd
        def _(pool):
            pool.memset(ones[:], 1.0).then_inc(consts_set, 1)
            pool.memset(eps[:], EPS).then_inc(consts_set, 1)
            for name, n in CREDIT.items():
                pool.sem_inc(sem[name], n)
            pool.sem_inc(stored["u"], 16)
            with pool.Fori(0, N_UNITS // 2) as i:
                for s in range(2):
                    pool.wait_ge(landed[s], 16 * i + 16)
                    pool.wait_ge(sem["unit_started"], 2 * i + (s + 1))
                    pool.sem_inc(gate_sem["pool"], 1)
                    pool.tensor_scalar(w_hi[:, s, :], w_raw[:, s, :], 1.0, 0.0, ALU.mult, ALU.add).then_inc(pool_hi, 1)
                    pool.wait_ge(pool_hi, 2 * i + (s + 1))
                    pool.tensor_tensor(w_lo[:, s, :], w_raw[:, s, :], w_hi[:, s, :].bitcast(F32), ALU.subtract
                                       ).then_inc(sem["unit_split"], 1)

        @block.tensor
        def _(pe):
            def past_waits():
                pe.sem_inc(gate_sem["pe"], 1)

            def sums(name):
                tiles = norms[name][2]
                for t, (a, b) in enumerate(tiles):
                    for half in range(2):
                        pe.wait_ge(sem["squared"], at("squared", name, 0, 2 * t + half + 1))
                        for c in range(4 * half, 4 * half + 4):
                            mm = pe.matmul(sum_banks[t][:, 0:b - a], ones[:], sq[:, t % 2, c, 0:b - a],
                                           start=(c == 0), stop=(c == CH - 1))
                    mm.then_inc(sem["summed"], 1)

            def enter(phase):
                pe.wait_ge(sem["freed_act"], at("freed_act", phase))
                pe.wait_ge(sem["freed_dve"], at("freed_dve", phase))

            def passes(out, slot, terms, unit_first=False, last_inc=True):
                todo = [(w, a) for cols, hi, lo in terms
                        for w, a in ((w_hi[:, slot, cols], hi), (w_hi[:, slot, cols], lo), (w_lo[:, slot, cols], hi))]
                for j, (w, a) in enumerate(todo):
                    mm = pe.matmul(out, w, a, start=(j == 0), stop=(j == len(todo) - 1))
                    if unit_first and j == 0:
                        mm.then_inc(sem["unit_started"], 1)
                mm.then_inc(sem["tile_done"], 1)

            def unit(phase, turn, u, p, tiles, hi, lo, ready=None):
                pe.wait_ge(sem["unit_split"], at("unit_split", phase, turn, u + 1))
                for t, (a, b) in enumerate(tiles):
                    bank = tile_plan(phase)[p][0]
                    name, value = bank_wait(phase, turn, p)
                    pe.wait_ge(sem[name], value)
                    if ready:
                        pe.wait_ge(sem["lo_ready"], at("lo_ready", ready, 0, 2 * t + 2))
                    passes(lin[bank][:, 0:b - a], u % 2,
                           [(slice(P * k, P * k + P), hi[:, k, a:b], lo[:, k, a:b]) for k in range(CH)],
                           unit_first=(t == 0))
                    p += 1
                return p

            def turn_values(phase, turn, k, v, n, new):
                pe.wait_ge(sem["freed_act"], n)
                pe.wait_ge(sem["mixed_out"], at("mixed_out", *new))
                for b in range(QB):
                    pe.transpose(ps_t[:, P * b:P * b + P], v[:, P * b:P * b + P], ident[:])
                pe.transpose(ps_o[0:BATCH_S, 0:P], v[:, SEQ:TOK], ident[:]).then_inc(sem["v_turned"], 1)

            def attention(phase, turn, kind, n, q, k, vnat, vnew, qd, p, pt, ps, ks, vs, part=0, slots=None):
                jobs_before = part * (n + 1)
                pe.wait_ge(sem["v_ready"], at("v_ready", "kv0" if kind == "swa" else phase,
                                              0 if kind == "swa" else turn, 1 if kind == "swa" else part + 1))
                freed = "exped" if kind == "mem" else "peaked"
                for what, job in pipeline(n):
                    s, t = jobs_before + order_s(job), jobs_before + order_t(job, n)
                    if what == "S":
                        pe.wait_ge(sem[freed], at(freed, phase, turn, s))
                        if job == "sample":
                            pe.wait_ge(sem["q_spread"], at("q_spread", phase, turn, part + 1))
                            if slots is not None:
                                pe.wait_ge(loads["k_slot"], slots)
                            past_waits()
                            if kind == "mem":
                                todo = [(ps_s[0:8, 0:256], qd[:, c, b, :], ks[:, b, c, :])
                                        for b in range(BATCH_S) for c in range(2)]
                            else:
                                nk = ks.shape[2]
                                todo = [(ps_s[0:16, 0:nk], qd[:, b, :], ks[:, b, :]) for b in range(BATCH_S)]
                                todo += [(ps_s[0:16, nk:nk + 1], qd[:, b, :], k[:, SEQ + b:SEQ + b + 1])
                                         for b in range(BATCH_S)]
                            for j, (o, w, a) in enumerate(todo):
                                mm = pe.matmul(o, w, a, start=(j == 0), stop=(j == len(todo) - 1), skip_group_check=True)
                        elif kind == "mem":
                            for c in range(2):
                                mm = pe.matmul(ps_s[:, 0:MEM], q[:, c, P * job:P * job + P], k[:, c, :],
                                               start=(c == 0), stop=(c == 1))
                        else:
                            kb, nb = key_blocks(kind, job)
                            r, qb = HEAD * (job // QB), job % QB
                            for o in range(0, nb * P, 512):
                                w = min(512, nb * P - o)
                                mm = pe.matmul(ps_s[:, o:o + w], q[r:r + HEAD, P * qb:P * qb + P],
                                               k[r:r + HEAD, P * kb + o:P * kb + o + w], start=True, stop=True)
                        mm.then_inc(sem["scored"], 1)
                    elif what == "T":
                        pe.wait_ge(sem["normed"], at("normed", phase, turn, s + 1))
                        past_waits()
                        if job == "sample":
                            rows = 8 if kind == "mem" else 16
                            nkb = 2 if kind == "mem" else ks.shape[2] // P
                            for b in range(nkb):
                                mm = pe.transpose(ps_t[:, rows * b:rows * b + rows], ps[:, P * b:P * b + P],
                                                  ident[0:rows, 0:rows])
                            if kind != "mem":
                                mm = pe.transpose(ps_t[0:BATCH_S, 512:528], sel[kind][:], ident[0:rows, 0:rows])
                        else:
                            for b in range(key_blocks(kind, job)[1]):
                                mm = pe.transpose(ps_t[:, P * b:P * b + P], p[:, job % 2, P * b:P * b + P], ident[:])
                        mm.then_inc(sem["turned"], 1)
                    else:
                        pe.wait_ge(sem["turned_in"], at("turned_in", phase, turn, t + 1))
                        pe.wait_ge(sem["mixed_out"], at("mixed_out", phase, turn, t))
                        if job == "sample":
                            if slots is not None:
                                pe.wait_ge(loads["v_slot"], slots)
                            past_waits()
                            if kind == "mem":
                                todo = [(ps_o[:, 8 * c + b:8 * c + b + 1], vs[:, b, m, P * c:P * c + P],
                                         pt[:, 8 * m + b:8 * m + b + 1])
                                        for b in range(BATCH_S) for c in range(2) for m in range(2)]
                            else:
                                nkb = ks.shape[2] // P
                                todo = [(ps_o[:, 0:16], vnew[:, :], pt[0:BATCH_S, 16 * nkb:16 * nkb + 16])]
                                todo += [(ps_o[:, 2 * b:2 * b + 2], vs[:, b, m, :],
                                          pt[:, 16 * m + 2 * b:16 * m + 2 * b + 2])
                                         for b in range(BATCH_S) for m in range(nkb)]
                            for j, (o, w, a) in enumerate(todo):
                                mm = pe.matmul(o, w, a, start=(j == 0), stop=(j == len(todo) - 1), skip_group_check=True)
                        elif kind == "mem":
                            for c in range(2):
                                for m in range(2):
                                    mm = pe.matmul(ps_o[:, P * c:P * c + P], vnat[:, m, P * c:P * c + P],
                                                   pt[:, P * m:P * m + P], start=(m == 0), stop=(m == 1))
                        else:
                            kb, nb = key_blocks(kind, job)
                            r = HEAD * (job // QB)
                            for m in range(nb):
                                mm = pe.matmul(ps_o[r:r + HEAD, 0:P], vnat[:, kb + m, r:r + HEAD],
                                               pt[:, P * m:P * m + P], start=(m == 0), stop=(m == nb - 1))
                        mm.then_inc(sem["mixed"], 1)

            def linear_out(phase, ready):
                enter(phase)
                with pe.Fori(0, 4) as i:
                    p = 0
                    for u in range(2):
                        p = unit(phase, i, u, p, TILES, h_hi, h_lo, ready if u == 0 else None)

            def cross(l):
                ph = f"cross{l}"
                pe.wait_ge(sem["lo_ready"], at("lo_ready", f"norm_mem{l}", 0, 2))
                enter(ph)
                with pe.Fori(0, CA_HEADS) as i:
                    p = 0
                    for u in range(4):
                        p = unit(ph, i, u, p, [(0, MEM)], mem_hi, mem_lo)
                    p = unit(ph, i, 4, p, TILES, h_hi, h_lo, f"norm_ca{l}")
                    p = unit(ph, i, 5, p, TILES, h_hi, h_lo)
                    pe.wait_ge(sem["freed_act"], at("freed_act", ph, i, 4))
                    for c in range(2):
                        for m in range(2):
                            mm = pe.transpose(ps_t[:, MEM * m + P * c:MEM * m + P * c + P], vc[:, c, P * m:P * m + P], ident[:])
                    mm.then_inc(sem["v_turned"], 1)
                    pe.wait_ge(sem["freed_act"], at("freed_act", ph, i, 10))
                    attention(ph, i, "mem", QB, qc, kc, vnatc, None, qdc, p_c, ptc, psc,
                              kv_slotc[:, :].rearrange("p (b c n) -> p b c n", b=BATCH_S, c=2),
                              kv_slotc[:, :].rearrange("p (b m d) -> p b m d", b=BATCH_S, m=2),
                              slots=slot_value(l, 1, i))

            def ffn(l):
                ph = f"ffn{l}"
                enter(ph)
                with pe.Fori(0, FFN_STEPS) as i:
                    p = 0
                    for u in range(4):
                        p = unit(ph, i, u, p, TILES, h_hi, h_lo, f"norm_ffn{l}" if u == 0 else None)
                    for u in range(4, 6):
                        pe.wait_ge(sem["unit_split"], at("unit_split", ph, i, u + 1))
                        for t, (a, b) in enumerate(TILES):
                            pe.wait_ge(sem["hid_lo"], at("hid_lo", ph, i, 3 + t + 1))
                            for n in range(4):
                                name, value = bank_wait(ph, i, p)
                                pe.wait_ge(sem[name], value)
                                passes(lin[tile_plan(ph)[p][0]][:, 0:b - a], u % 2,
                                       [(slice(512 * k + P * n, 512 * k + P * n + P), hid_hi[:, k, a:b], hid_lo[:, k, a:b])
                                        for k in range(2)], unit_first=(t == 0 and n == 0))
                                p += 1

            pe.wait_ge(loads["consts"], 48)
            pe.wait_ge(consts_set, 2)
            sums("norm_mix0")
            enter("kv0")
            p = unit("kv0", 0, 0, 0, TILES, h_hi, h_lo, "norm_mix0")
            p = unit("kv0", 0, 1, p, TILES, h_hi, h_lo)
            turn_values("kv0", 0, k0, v0, at("freed_act", "kv0", 0, 6), ("att0", 0, 0))
            enter("att0")
            pe.wait_ge(loads["att0"], ATT0_LOADS)
            with pe.Fori(0, PAIRS) as i:
                p = 0
                for u in range(4):
                    p = unit("att0", i, u, p, TILES, h_hi, h_lo)
                pe.wait_ge(sem["freed_act"], at("freed_act", "att0", i, 3))
                attention("att0", i, "swa", 2 * QB, q0, k0, vnat0, vnew0, qd0, p0, pt0, ps0, ks0, vs0)
            linear_out("out0", "split0")
            sums("norm_mem0")
            sums("norm_ca0")
            cross(0)
            linear_out("caout0", "casplit0")
            sums("norm_ffn0")
            ffn(0)
            sums("norm_mix1")
            enter("pool1")
            pe.wait_ge(loads["pool1"], 64)

            def pool_map(g):
                pe.wait_ge(sem["delta_ready"], at("delta_ready", "pool1", 0, g + 1))
                for t, (a, b) in enumerate(TILES):
                    if g:
                        pe.wait_ge(sem["pooled_out"], at("pooled_out", "pool1", 0, 3 * (g - 1) + t + 1))
                    pe.matmul(sum_banks[t][:, 0:b - a], pool_w[:, g, :], pool_d[:, g % 2, a:b], start=True, stop=True
                              ).then_inc(sem["pooled"], 1)

            p = 0
            for g in range(4):
                p = unit("pool1", 0, g, p, TILES, h_hi, h_lo, "norm_mix1" if g == 0 else None)
                if g:
                    pool_map(g - 1)
            pool_map(3)
            enter("att1")
            pe.wait_ge(sem["pooled_out"], at("pooled_out", "pool1", 0, 12))
            with pe.Fori(0, PAIRS // 2) as i:
                p = 0
                for part in range(2):
                    for u in range(3):
                        p = unit("att1", i, 3 * part + u, p, TILES, h_hi, h_lo)
                    turn_values("att1", i, k1, v1, at("freed_act", "att1", i, 9 * part + 9),
                                ("att1", i, part * (2 * QB + 1)))
                    attention("att1", i, "dil", 2 * QB, q1, k1, vnat1, vnew1, qd1, p1, pt1, ps1,
                              kv_slot1[:, :].rearrange("p (b n) -> p b n", b=BATCH_S),
                              kv_slot1[:, :].rearrange("p (b m d) -> p b m d", b=BATCH_S, m=3), part=part,
                              slots=slot_value(1, 0, i, part))
            linear_out("out1", "split1")
            sums("norm_mem1")
            sums("norm_ca1")
            cross(1)
            linear_out("caout1", "casplit1")
            sums("norm_ffn1")
            ffn(1)
            sums("norm_final")

        @block.scalar
        def _(act):
            def past_waits():
                act.sem_inc(gate_sem["act"], 1)

            def copy(out, in_, **kw):
                return act.activation(out, in_, ACT.Copy, **kw)

            def norm(name):
                _, src, tiles, hi, _ = norms[name]
                split = hi is not None

                def squares(t):
                    a, b = tiles[t]
                    if t >= 2:
                        act.wait_ge(sem["summed"], at("summed", name, 0, t - 1))
                    for half in range(2):
                        c = slice(4 * half, 4 * half + 4)
                        act.activation(sq[:, t % 2, c, 0:b - a], src[:, c, a:b], ACT.Square).then_inc(sem["squared"], 1)

                def roots(t):
                    a, b = tiles[t]
                    if t >= 2:
                        act.wait_ge(sem["rsqrted"], at("rsqrted", name, 0, t - 1))
                    act.wait_ge(sem["summed"], at("summed", name, 0, t + 1))
                    act.activation(root[:, t % 2, 0:b - a], sum_banks[t][:, 0:b - a], ACT.Sqrt, bias=eps[:, 0:1],
                                   scale=1.0 / D).then_inc(sem["rooted"], 1)

                def rounded(t):
                    a, b = tiles[t]
                    for half in range(2):
                        c = slice(4 * half, 4 * half + 4)
                        act.wait_ge(sem["scaled"], at("scaled", name, 0, 2 * t + half + 1))
                        copy(hi[:, c, a:b], scaled[:, t % 2, c, 0:b - a]).then_inc(sem["hi_ready"], 1)

                for t in range(len(tiles)):
                    squares(t)
                    if t:
                        roots(t - 1)
                roots(len(tiles) - 1)
                if split:
                    for t in range(len(tiles)):
                        rounded(t)

            def split(phase, mix, before):
                act.wait_ge(sem["mixed_out"], at("mixed_out", phase))
                act.wait_ge(sem["freed_dve"], at("freed_dve", phase))
                act.wait_ge(sem["tile_done"], at("tile_done", phase))
                for t, (a, b) in enumerate(TILES):
                    for half in range(2):
                        c = slice(4 * half, 4 * half + 4)
                        copy(h_hi[:, c, a:b], mix[:, c, a:b]).then_inc(sem["hi_ready"], 1)

            def empty(phase, turn, p, out, w=TILE):
                act.wait_ge(sem["tile_done"], at("tile_done", phase, turn, p + 1))
                copy(out, lin[tile_plan(phase)[p][0]][:, 0:w]).then_inc(sem["freed_act"], 1)

            def values_in(vnat, vnew, phase, turn, k):
                act.wait_ge(sem["v_turned"], at("v_turned", phase, turn, k + 1))
                copy(vnat[:, :, :], ps_t[:, 0:1024].rearrange("p (b d) -> p b d", b=QB))
                copy(vnew[:, :], ps_o[0:BATCH_S, 0:P]).then_inc(sem["v_ready"], 1)

            def attention(phase, turn, kind, n, mix, chunk, p, pt, ps, part=0, values=None):
                before = part * (n + 1)
                scale = 1.0 / 16.0 if kind == "mem" else 1.0 / 8.0
                nkb = {"swa": 1, "dil": 3, "mem": 2}[kind]
                rows = 8 if kind == "mem" else 16
                for what, job in pipeline(n):
                    s, t = before + order_s(job), before + order_t(job, n)
                    o = order_s(job) % 2
                    if what == "S":
                        m = rows if job == "sample" else P
                        if kind == "mem":
                            src = ps_s[0:m, 0:MEM]
                            dst = ps[:, :] if job == "sample" else p[:, job % 2, :]
                        elif job == "sample":
                            src = dst = ps[:, :]
                        else:
                            src = dst = p[:, job % 2, 0:P * key_blocks(kind, job)[1]]
                        act.wait_ge(sem["biased"], at("biased", phase, turn, s + 1))
                        if kind == "swa":
                            c = 2 if job == "sample" else job // QB
                            act.activation(sink_exp[0:m, o:o + 1], sink8[0:m, c:c + 1], ACT.Exp, scale=scale,
                                           bias=bias[0:m, o:o + 1])
                        act.activation(dst, src, ACT.Exp, scale=scale, bias=bias[0:m, o:o + 1],
                                       accum_out=den[0:m, o:o + 1]).then_inc(sem["exped"], 1)
                        if job == "sample" and values is not None:
                            slot, src_v = values
                            act.dma_start(slot, src_v).then_inc(loads["v_slot"], 16)
                    elif what == "T":
                        act.wait_ge(sem["turned"], at("turned", phase, turn, t + 1))
                        if job == "sample":
                            mm = copy(pt[:, 0:rows * nkb], ps_t[:, 0:rows * nkb])
                            if kind != "mem":
                                mm = copy(pt[0:BATCH_S, 16 * nkb:16 * nkb + 16], ps_t[0:BATCH_S, 512:528])
                        else:
                            w = P * key_blocks(kind, job)[1]
                            mm = copy(pt[:, 0:w], ps_t[:, 0:w])
                        mm.then_inc(sem["turned_in"], 1)
                    else:
                        act.wait_ge(sem["mixed"], at("mixed", phase, turn, t + 1))
                        past_waits()
                        if kind == "mem":
                            a, w = (SEQ, 8) if job == "sample" else (P * job, P)
                            mm = copy(mix[:, bass.ds(chunk, 2), a:a + w],
                                      ps_o[:, 0:2 * w].rearrange("p (c n) -> p c n", c=2))
                        elif job == "sample":
                            copy(mix[0:HEAD, bass.ds(chunk, 1), SEQ:TOK], ps_o[0:HEAD, 0:16:2].rearrange("p (a n) -> p a n", a=1))
                            mm = copy(mix[HEAD:P, bass.ds(chunk, 1), SEQ:TOK],
                                      ps_o[HEAD:P, 1:16:2].rearrange("p (a n) -> p a n", a=1))
                        else:
                            r, qb = HEAD * (job // QB), job % QB
                            mm = copy(mix[r:r + HEAD, bass.ds(chunk, 1), P * qb:P * qb + P],
                                      ps_o[r:r + HEAD, 0:P].rearrange("p (a n) -> p a n", a=1))
                        mm.then_inc(sem["mixed_out"], 1)

            def cross(l):
                ph = f"cross{l}"
                with act.Fori(0, CA_HEADS) as i:
                    act.wait_ge(stored["k"], stored_before(l, 1, i))
                    for c in range(2):
                        empty(ph, i, c, kc[:, c, :], MEM)
                    act.wait_ge(stored["v"], stored_before(l, 1, i))
                    for c in range(2):
                        empty(ph, i, 2 + c, vc[:, c, :], MEM)
                    act.wait_ge(sem["freed_act"], at("freed_act", ph, i, 4))
                    act.dma_start(dram["mem_k"][l, bass.ds(i, 1)].rearrange("a p c n -> p (a c) n"), kc[:]).then_inc(stored["k"], 16)
                    act.dma_start(dram["mem_v"][l, bass.ds(i, 1)].rearrange("a p c n -> p (a c) n"), vc[:]).then_inc(stored["v"], 16)
                    act.wait_ge(sem["lo_ready"], at("lo_ready", f"norm_ca{l}", 0, 6))
                    act.dma_start(kv_slotc[:, :], dram["mem_cache_k"][l, bass.ds(i, 1)].rearrange("a p n -> p (a n)")
                                  ).then_inc(loads["k_slot"], 16)
                    for u in range(2):
                        for t, (a, b) in enumerate(TILES):
                            empty(ph, i, 4 + 3 * u + t, qc[:, u, a:b])
                    act.wait_ge(sem["v_turned"], at("v_turned", ph, i, 1))
                    copy(vnatc[:, :, :], ps_t[:, 0:512].rearrange("p (m d) -> p m d", m=2)).then_inc(sem["v_ready"], 1)
                    attention(ph, i, "mem", QB, mixc, 2 * i, p_c, ptc, psc,
                              values=(kv_slotc[:, :], dram["mem_cache_v"][l, bass.ds(i, 1)].rearrange("a p n -> p (a n)")))
                split(f"casplit{l}", mixc, ph)

            def ffn(l):
                ph = f"ffn{l}"
                with act.Fori(0, FFN_STEPS) as i:
                    for c in range(2):
                        for t, (a, b) in enumerate(TILES):
                            p = 6 * c + t
                            act.wait_ge(sem["tile_done"], at("tile_done", ph, i, p + 1))
                            act.activation(gate[:, a:b], lin[tile_plan(ph)[p][0]][:, 0:TILE], ACT.Silu
                                           ).then_inc(sem["freed_act"], 1)
                        for t, (a, b) in enumerate(TILES):
                            act.wait_ge(sem["freed_dve"], at("freed_dve", ph, i, 3 * c + t + 1))
                            copy(hid_hi[:, c, a:b], hid[:, a:b]).then_inc(sem["hid_hi"], 1)

            act.wait_ge(loads["x"], 16)
            act.wait_ge(consts_set, 2)
            norm("norm_mix0")
            act.wait_ge(sem["lo_ready"], at("lo_ready", "norm_mix0", 0, 6))
            for dst, name in ((ks0, "swa_k"), (vs0, "swa_v"), (stash, "stash"), (mask0, "mask0"), (smask0, "smask0")):
                act.dma_start(dst[:], dram[name]).then_inc(loads["att0"], 16)
            for t, (a, b) in enumerate(TILES):
                empty("kv0", 0, t, k0[:, a:b])
            for t, (a, b) in enumerate(TILES):
                empty("kv0", 0, 3 + t, v0[:, a:b])
            act.wait_ge(sem["freed_act"], at("freed_act", "kv0", 0, 6))
            act.dma_start(dram["swa_k_out"], k0[:, SEQ - P:TOK]).then_inc(stored["k"], 16)
            act.dma_start(dram["swa_v_out"], v0[:, SEQ - P:TOK]).then_inc(stored["v"], 16)
            values_in(vnat0, vnew0, "kv0", 0, 0)
            with act.Fori(0, PAIRS) as i:
                for t, (a, b) in enumerate(TILES):
                    empty("att0", i, t, q0[:, a:b])
                for t, (a, b) in enumerate(TILES):
                    empty("att0", i, 3 + t, cgate[:, a:b])
                act.wait_ge(sem["freed_dve"], at("freed_dve", "att0", i, 3))
                act.dma_start(dram["conv_out"][bass.ds(i, 1)].rearrange("a p n -> p (a n)"), conv_u[:, SEQ:2 + TOK]
                              ).then_inc(stored["u"], 16)
                attention("att0", i, "swa", 2 * QB, mix0, i + 4, p0, pt0, ps0)
            split("split0", mix0, "att0")

            def memory_and_ca(l):
                act.wait_ge(sem["freed_dve"], at("freed_dve", f"norm_mem{l}"))
                act.dma_start(mem_in[:], dram["mem"]).then_inc(loads[f"mem{l}"], 16)
                act.wait_ge(loads[f"mem{l}"], 16)
                norm(f"norm_mem{l}")
                act.wait_ge(sem["lo_ready"], at("lo_ready", f"norm_mem{l}", 0, 2))
                norm(f"norm_ca{l}")

            memory_and_ca(0)
            cross(0)
            act.wait_ge(sem["freed_dve"], at("freed_dve", "norm_ffn0"))
            norm("norm_ffn0")
            ffn(0)
            act.wait_ge(sem["freed_dve"], at("freed_dve", "norm_mix1"))
            norm("norm_mix1")
            act.wait_ge(sem["lo_ready"], at("lo_ready", "norm_mix1", 0, 6))
            for dst, name in ((pool_hist, "pool_hist"), (pool_w, "pool_w"), (pool_rcp, "pool_rcp"), (pool_gain, "pool_gain")):
                act.dma_start(dst[:], dram[name]).then_inc(loads["pool1"], 16)
            act.wait_ge(loads["pool1"], 64)

            def pool_out(g):
                for t, (a, b) in enumerate(TILES):
                    act.wait_ge(sem["pooled"], at("pooled", "pool1", 0, 3 * g + t + 1))
                    copy(mix1[:, g, a:b], sum_banks[t][:, 0:TILE], scale=pool_gain[:, g:g + 1]
                         ).then_inc(sem["pooled_out"], 1)

            for g in range(4):
                if g:
                    act.wait_ge(sem["delta_ready"], at("delta_ready", "pool1", 0, g))
                    act.wait_ge(stored["u"], 16 * (PAIRS + g + 1))
                for t, (a, b) in enumerate(TILES):
                    empty("pool1", 0, 3 * g + t, pool_u[:, POOL_PAD + a:POOL_PAD + b])
                act.wait_ge(sem["freed_act"], at("freed_act", "pool1", 0, 3 * g + 3))
                act.dma_start(dram["pool_out"][g], pool_u[:, SEQ:POOL_PAD + TOK]).then_inc(stored["u"], 16)
                if g:
                    pool_out(g - 1)
            pool_out(3)
            act.wait_ge(stored["u"], 16 * (PAIRS + 5))
            act.wait_ge(sem["pooled_out"], at("pooled_out", "pool1", 0, 12))
            act.dma_start(mask1[:], dram["mask1"]).then_inc(loads["att1"], 16)
            act.dma_start(smask1[:], dram["smask1"]).then_inc(loads["att1"], 16)
            with act.Fori(0, PAIRS // 2) as i:
                for part in range(2):
                    act.dma_start(kv_slot1[:, :], dram["dil_k"][bass.ds(2 * i + part, 1)].rearrange("a p n -> p (a n)")
                                  ).then_inc(loads["k_slot"], 16)
                    for t, (a, b) in enumerate(TILES):
                        empty("att1", i, 9 * part + t, q1[:, a:b])
                    act.wait_ge(stored["k"], stored_before(1, 0, i, part))
                    for t, (a, b) in enumerate(TILES):
                        empty("att1", i, 9 * part + 3 + t, k1[:, a:b])
                    act.wait_ge(stored["v"], stored_before(1, 0, i, part))
                    for t, (a, b) in enumerate(TILES):
                        empty("att1", i, 9 * part + 6 + t, v1[:, a:b])
                    act.wait_ge(sem["freed_act"], at("freed_act", "att1", i, 9 * part + 9))
                    act.dma_start(dram["dil_k_out"][bass.ds(2 * i + part, 1)].rearrange("a p n -> p (a n)"), k1[:, :]
                                  ).then_inc(stored["k"], 16)
                    act.dma_start(dram["dil_v_out"][bass.ds(2 * i + part, 1)].rearrange("a p n -> p (a n)"), v1[:, :]
                                  ).then_inc(stored["v"], 16)
                    values_in(vnat1, vnew1, "att1", i, part)
                    attention("att1", i, "dil", 2 * QB, mix1, 2 * i + (4 + part), p1, pt1, ps1, part=part,
                              values=(kv_slot1[:, :], dram["dil_v"][bass.ds(2 * i + part, 1)].rearrange("a p n -> p (a n)")))
            split("split1", mix1, "att1")
            memory_and_ca(1)
            cross(1)
            act.wait_ge(sem["freed_dve"], at("freed_dve", "norm_ffn1"))
            norm("norm_ffn1")
            ffn(1)
            act.wait_ge(sem["freed_dve"], at("freed_dve", "norm_final"))
            norm("norm_final")
            for t, (a, b) in enumerate(TILES):
                act.wait_ge(sem["scaled"], at("scaled", "norm_final", 0, 2 * t + 2))
                act.dma_start(dram["y"][:, :, a:b], scaled[:, t % 2, :, 0:b - a]).then_inc(stored[f"y{t}"], 16)
            act.wait_ge(stored["k"], KV_STORES)
            act.wait_ge(stored["v"], KV_STORES)
            act.wait_ge(stored["u"], 16 * (PAIRS + 5))
            for t in range(3):
                act.wait_ge(stored[f"y{t}"], 16)

        @block.vector
        def _(dve):
            steps = [0]

            def past_waits():
                dve.sem_inc(gate_sem["dve"], 1)

            def norm(name):
                gain, src, tiles, hi, lo = norms[name]
                g = GAINS.index(gain)
                split = hi is not None
                for t, (a, b) in enumerate(tiles):
                    w = b - a
                    dve.wait_ge(sem["rooted"], at("rooted", name, 0, t + 1))
                    dve.reciprocal(rsqrt[:, t % 2, 0:w], root[:, t % 2, 0:w]).then_inc(sem["rsqrted"], 1)
                    dve.wait_ge(sem["rsqrted"], at("rsqrted", name, 0, t + 1))
                    if not split and t >= 2:
                        dve.wait_ge(stored[f"y{t - 2}"], 16)
                    for c in range(CH):
                        op = dve.scalar_tensor_tensor(scaled[:, t % 2, c, 0:w], src[:, c, a:b], gains[:, g, c:c + 1],
                                                      rsqrt[:, t % 2, 0:w], ALU.mult, ALU.mult)
                        if c % 4 == 3:
                            op.then_inc(sem["scaled"], 1)
                    for half in range(2 if split else 0):
                        c = slice(4 * half, 4 * half + 4)
                        dve.wait_ge(sem["hi_ready"], at("hi_ready", name, 0, 2 * t + half + 1))
                        dve.tensor_tensor(lo[:, c, a:b], scaled[:, t % 2, c, 0:w], hi[:, c, a:b].bitcast(F32), ALU.subtract
                                          ).then_inc(sem["lo_ready"], 1)

            def split(phase, mix):
                for t, (a, b) in enumerate(TILES):
                    for half in range(2):
                        c = slice(4 * half, 4 * half + 4)
                        dve.wait_ge(sem["hi_ready"], at("hi_ready", phase, 0, 2 * t + half + 1))
                        dve.tensor_tensor(h_lo[:, c, a:b], mix[:, c, a:b], h_hi[:, c, a:b].bitcast(F32), ALU.subtract
                                          ).then_inc(sem["lo_ready"], 1)

            def linear_out(phase):
                with dve.Fori(0, 4) as i:
                    for u in range(2):
                        for t, (a, b) in enumerate(TILES):
                            p = 3 * u + t
                            dve.wait_ge(sem["tile_done"], at("tile_done", phase, i, p + 1))
                            xs = x[:, bass.ds(2 * i + u, 1), a:b].rearrange("p a n -> p (a n)")
                            dve.tensor_tensor(xs, lin[tile_plan(phase)[p][0]][:, 0:TILE], xs, ALU.add
                                              ).then_inc(sem["freed_dve"], 1)

            def attention(phase, turn, kind, n, p, ps, mask, smask, part=0):
                before = part * (n + 1)
                scale = 1.0 / 16.0 if kind == "mem" else 1.0 / 8.0
                rows = 8 if kind == "mem" else 16
                for what, job in pipeline(n):
                    if what != "S":
                        continue
                    s = before + order_s(job)
                    o = order_s(job) % 2
                    m = rows if job == "sample" else P
                    dve.wait_ge(sem["scored"], at("scored", phase, turn, s + 1))
                    dve.wait_ge(sem["turned"], at("turned", phase, turn, before + (0 if job == "sample" or job < 2 else job - 1)))
                    if kind == "mem":
                        dst = ps[:, :] if job == "sample" else p[:, job % 2, :]
                        dve.tensor_reduce(peak[0:m, o:o + 1], ps_s[0:m, 0:MEM], AX_X, ALU.max).then_inc(sem["peaked"], 1)
                    else:
                        past_waits()
                        if job == "sample":
                            w, dst, msk = ps.shape[1], ps[:, :], smask[:, :]
                        else:
                            w = P * key_blocks(kind, job)[1]
                            dst, msk = p[:, job % 2, 0:w], mask[:, mask.shape[1] - w:]
                        start = NEG
                        if kind == "swa":
                            c = 2 if job == "sample" else job // QB
                            start = sink8[0:m, c:c + 1]
                        dve.tensor_tensor_reduce(dst, ps_s[0:m, 0:w], msk, 1.0, start, ALU.add, ALU.max,
                                                 peak[0:m, o:o + 1]).then_inc(sem["peaked"], 1)
                    dve.wait_ge(sem["peaked"], at("peaked", phase, turn, s + 1))
                    dve.tensor_scalar(bias[0:m, o:o + 1], peak[0:m, o:o + 1], -scale, None, ALU.mult).then_inc(sem["biased"], 1)
                    dve.wait_ge(sem["exped"], at("exped", phase, turn, s + 1))
                    total = den
                    if kind == "swa":
                        dve.tensor_tensor(peak[0:m, o:o + 1], den[0:m, o:o + 1], sink_exp[0:m, o:o + 1], ALU.add
                                          ).then_inc(dve_step, 1)
                        dve.wait_ge(dve_step, turn * DVE_PER_TURN + (DVE_BASE + CONV_STEPS + s + 1))
                        total = peak
                    dve.reciprocal(inv[0:m, o:o + 1], total[0:m, o:o + 1]).then_inc(sem["inverted"], 1)
                    dve.wait_ge(sem["inverted"], at("inverted", phase, turn, s + 1))
                    if job != "sample" or kind == "mem":
                        dve.tensor_scalar(dst, dst, inv[0:m, o:o + 1], None, ALU.mult).then_inc(sem["normed"], 1)
                    else:
                        w = ps.shape[1]
                        dve.tensor_scalar(sel[kind][:], token_mask[:], ps[:, w - 1:w], inv[0:m, o:o + 1], ALU.mult, ALU.mult)
                        dve.tensor_scalar(ps[:, 0:w - 1], ps[:, 0:w - 1], inv[0:m, o:o + 1], None, ALU.mult
                                          ).then_inc(sem["normed"], 1)

            def spread(q, qd, ph, turn, part, at_freed):
                dve.wait_ge(sem["freed_act"], at_freed)
                past_waits()
                flat = qd[:, :, :].rearrange("p b n -> p (b n)")
                dve.tensor_copy(flat[0:HEAD, 0:P:18], q[0:HEAD, SEQ:TOK])
                dve.tensor_copy(flat[HEAD:P, 1:P:18], q[HEAD:P, SEQ:TOK]).then_inc(sem["q_spread"], 1)

            def cross(l):
                ph = f"cross{l}"
                dve.memset(qdc[:], 0.0).then_inc(dve_step, 1)
                dve.wait_ge(dve_step, CROSS_STEP[l])
                with dve.Fori(0, CA_HEADS) as i:
                    dve.wait_ge(sem["freed_act"], at("freed_act", ph, i, 10))
                    past_waits()
                    for c in range(2):
                        op = dve.tensor_copy(qdc[:, c, :, :].rearrange("p b n -> p (b n)")[:, 0:64:9], qc[:, c, SEQ:TOK])
                    op.then_inc(sem["q_spread"], 1)
                    attention(ph, i, "mem", QB, p_c, psc, None, None)
                split(f"casplit{l}", mixc)

            def ffn(l):
                ph = f"ffn{l}"
                with dve.Fori(0, FFN_STEPS) as i:
                    for c in range(2):
                        for t, (a, b) in enumerate(TILES):
                            p = 6 * c + 3 + t
                            dve.wait_ge(sem["tile_done"], at("tile_done", ph, i, p + 1))
                            dve.wait_ge(sem["freed_act"], at("freed_act", ph, i, 3 * c + t + 1))
                            dve.tensor_tensor(hid[:, a:b], lin[tile_plan(ph)[p][0]][:, 0:TILE], gate[:, a:b], ALU.mult
                                              ).then_inc(sem["freed_dve"], 1)
                            dve.wait_ge(sem["hid_hi"], at("hid_hi", ph, i, 3 * c + t + 1))
                            dve.tensor_tensor(hid_lo[:, c, a:b], hid[:, a:b], hid_hi[:, c, a:b].bitcast(F32), ALU.subtract
                                              ).then_inc(sem["hid_lo"], 1)
                    p = 12
                    for half in range(2):
                        for t, (a, b) in enumerate(TILES):
                            for n in range(4):
                                dve.wait_ge(sem["tile_done"], at("tile_done", ph, i, p + 1))
                                dve.tensor_tensor(x[:, 4 * half + n, a:b], lin[tile_plan(ph)[p][0]][:, 0:TILE],
                                                  x[:, 4 * half + n, a:b], ALU.add).then_inc(sem["freed_dve"], 1)
                                p += 1

            dve.wait_ge(loads["x"], 16)
            dve.wait_ge(loads["consts"], 48)
            norm("norm_mix0")
            dve.wait_ge(loads["att0"], ATT0_LOADS)
            dve.wait_ge(sem["lo_ready"], at("lo_ready", "norm_mix0", 0, 6))
            dve.memset(conv_u[:, 0:2], 0.0)
            dve.memset(qd0[:], 0.0).then_inc(dve_step, 1)
            dve.wait_ge(dve_step, 1)
            with dve.Fori(0, PAIRS) as i:
                def step(k):
                    dve.wait_ge(dve_step, i * DVE_PER_TURN + (DVE_BASE + k))

                dve.tensor_copy(cur[:], stash[:, bass.ds(i, 1), :].rearrange("p a n -> p (a n)")).then_inc(dve_step, 1)
                step(1)
                dve.tensor_scalar(sink8[:], cur[:, 19:22], 8.0, None, ALU.mult).then_inc(dve_step, 1)
                step(2)
                spread(q0, qd0, "att0", i, 0, at("freed_act", "att0", i, 3))
                dve.wait_ge(stored["u"], 16 * i + 16)
                for t, (a, b) in enumerate(TILES):
                    dve.wait_ge(sem["freed_act"], at("freed_act", "att0", i, 3 + t + 1))
                    dve.wait_ge(sem["tile_done"], at("tile_done", "att0", i, 6 + t + 1))
                    dve.tensor_tensor(conv_u[:, 2 + a:2 + b], lin[t][:, 0:TILE], cgate[:, a:b], ALU.mult
                                      ).then_inc(sem["freed_dve"], 1)
                dve.wait_ge(sem["freed_dve"], at("freed_dve", "att0", i, 3))
                past = lambda r: cur[:, 3 + 8 * r:11 + 8 * r]
                dve.tensor_scalar(conv_t[:, 0:SEQ], conv_u[:, 0:SEQ], cur[:, 0:1], None, ALU.mult)
                dve.tensor_scalar(conv_t[:, SEQ:TOK], past(0), cur[:, 0:1], None, ALU.mult).then_inc(dve_step, 1)
                step(3)
                dve.scalar_tensor_tensor(conv_t[:, 0:SEQ], conv_u[:, 1:SEQ + 1], cur[:, 1:2], conv_t[:, 0:SEQ], ALU.mult, ALU.add)
                dve.scalar_tensor_tensor(conv_t[:, SEQ:TOK], past(1), cur[:, 1:2], conv_t[:, SEQ:TOK], ALU.mult, ALU.add
                                         ).then_inc(dve_step, 1)
                step(4)
                dve.scalar_tensor_tensor(conv_t[:, :], conv_u[:, 2:2 + TOK], cur[:, 2:3], conv_t[:, :], ALU.mult, ALU.add
                                         ).then_inc(dve_step, 1)
                step(5)
                for t, (a, b) in enumerate(TILES):
                    dve.wait_ge(sem["tile_done"], at("tile_done", "att0", i, 9 + t + 1))
                    dve.tensor_tensor(mix0[:, bass.ds(i, 1), a:b].rearrange("p a n -> p (a n)"), lin[t][:, 0:TILE],
                                      conv_t[:, a:b], ALU.mult).then_inc(sem["freed_dve"], 1)
                attention("att0", i, "swa", 2 * QB, p0, ps0, mask0, smask0)
            split("split0", mix0)
            linear_out("out0")

            def memory_and_ca(l):
                dve.wait_ge(loads[f"mem{l}"], 16)
                dve.wait_ge(sem["freed_dve"], at("freed_dve", f"norm_mem{l}"))
                norm(f"norm_mem{l}")
                dve.wait_ge(sem["lo_ready"], at("lo_ready", f"norm_mem{l}", 0, 2))
                norm(f"norm_ca{l}")

            memory_and_ca(0)
            cross(0)
            linear_out("caout0")
            dve.wait_ge(sem["freed_dve"], at("freed_dve", "norm_ffn0"))
            norm("norm_ffn0")
            ffn(0)
            dve.wait_ge(sem["freed_dve"], at("freed_dve", "norm_mix1"))
            norm("norm_mix1")
            dve.wait_ge(loads["pool1"], 64)
            dve.wait_ge(sem["lo_ready"], at("lo_ready", "norm_mix1", 0, 6))
            steps[0] = POOL_STEP

            def chained(op):
                steps[0] += 1
                op.then_inc(dve_step, 1)
                dve.wait_ge(dve_step, steps[0])

            chained(dve.memset(pool_u[:, 0:POOL_PAD], 0.0))
            for g, w in enumerate(POOL_WINDOWS):
                dve.wait_ge(sem["freed_act"], at("freed_act", "pool1", 0, 3 * g + 3))
                if g >= 2:
                    dve.wait_ge(sem["pooled"], at("pooled", "pool1", 0, 3 * (g - 1)))
                src, n, have = pool_u, POOL_PAD + SEQ, 1
                for dst in (pool_a, pool_b, pool_a, pool_b)[:g + 1]:
                    n -= have
                    chained(dve.tensor_tensor(dst[:, 0:n], src[:, have:have + n], src[:, 0:n], ALU.add))
                    src, have = dst, 2 * have
                win = src[:, 16 - w:16 - w + SEQ]
                d = pool_d[:, g % 2, :]
                u = pool_u[:, POOL_PAD:]
                head = pool_s[:, :, :].rearrange("p a b -> p (a b)")
                dve.scalar_tensor_tensor(d[:, 16:SEQ], win[:, 16:SEQ], 1.0 / w, u[:, 16:SEQ], ALU.mult, ALU.subtract)
                chained(dve.tensor_tensor(head, win[:, 0:16], pool_rcp[:, g, :], ALU.mult))
                chained(dve.tensor_tensor(d[:, 0:16], head, u[:, 0:16], ALU.subtract))
                chained(dve.tensor_reduce(pool_s[:, 0, :], pool_hist[:, g, :, 16 - w:15], AX_X, ALU.add))
                chained(dve.tensor_tensor(pool_s[:, 1, :], pool_s[:, 0, :], u[:, SEQ:TOK], ALU.add))
                dve.scalar_tensor_tensor(d[:, SEQ:TOK], pool_s[:, 1, :], 1.0 / w, u[:, SEQ:TOK], ALU.mult, ALU.subtract
                                         ).then_inc(sem["delta_ready"], 1)
            dve.wait_ge(sem["pooled_out"], at("pooled_out", "pool1", 0, 12))
            dve.wait_ge(sem["delta_ready"], at("delta_ready", "pool1", 0, 4))
            chained(dve.memset(qd1[:], 0.0))
            assert steps[0] == ATT1_STEP
            dve.wait_ge(loads["att1"], 32)
            with dve.Fori(0, PAIRS // 2) as i:
                for part in range(2):
                    spread(q1, qd1, "att1", i, part, at("freed_act", "att1", i, 9 * part + 3))
                    attention("att1", i, "dil", 2 * QB, p1, ps1, mask1, smask1, part=part)
            split("split1", mix1)
            linear_out("out1")
            memory_and_ca(1)
            cross(1)
            linear_out("caout1")
            dve.wait_ge(sem["freed_dve"], at("freed_dve", "norm_ffn1"))
            norm("norm_ffn1")
            ffn(1)
            dve.wait_ge(sem["freed_dve"], at("freed_dve", "norm_final"))
            norm("norm_final")



def unit_list(i):
    def into(w, cols):
        return np.ascontiguousarray(w[:, cols].reshape(CH, P, P).transpose(1, 0, 2).reshape(P, D))

    def block(w, n):
        return into(w, slice(P * n, P * n + P))

    units = []
    pair_cols = [np.r_[HEAD * c:HEAD * c + HEAD, HEAD * (4 + c):HEAD * (4 + c) + HEAD] for c in range(PAIRS)]
    for l in range(2):
        if l == 0:
            w = i["w_in_even"][0]
            b0, c0, x0, q0, k0, v0 = 0, 512, 1024, 1536, 2048, 2176
            units += [block(w[:, k0:], 0), block(w[:, v0:], 0)]
            for c in range(PAIRS):
                units += [into(w, q0 + pair_cols[c]), block(w[:, c0:], c), block(w[:, x0:], c), block(w[:, b0:], c)]
            wo = i["w_out_even"][0]
            wo = np.concatenate([wo[:512]] + [wo[512 + pair_cols[c]] for c in range(PAIRS)])
        else:
            w = i["w_in_odd"][0]
            units += [block(w, g) for g in range(4)]
            for c in range(PAIRS):
                units += [block(w[:, o:], c) for o in (512, 1024, 1536)]
            wo = i["w_out_odd"][0]
        units += [block(wo, n) for n in range(CH)]
        wkv, wq = i["w_ca_kv"][l], i["w_ca_q"][l]
        for h in range(CA_HEADS):
            for w in (wkv[:, :D], wkv[:, D:], wq):
                units += [block(w, 2 * h), block(w, 2 * h + 1)]
        units += [block(i["w_ca_o"][l], n) for n in range(CH)]
        wi, wo = i["w_ffn_in"][l], i["w_ffn_out"][l]
        for s in range(FFN_STEPS):
            for n in (2 * s, 2 * s + 1):
                units += [block(wi, n), block(wi[:, FFN:], n)]
            rows = wo[256 * s:256 * s + 256].reshape(2, P, 2, 512)
            for half in range(2):
                units.append(np.ascontiguousarray(rows[:, :, half].transpose(1, 0, 2).reshape(P, D)))
    return np.stack(units)


def masks():
    def table(f, width):
        delta = (width - P) + np.arange(P)[:, None] - np.arange(width)[None, :]
        return f(delta).astype(np.float32)

    def window(delta):
        return np.where((delta >= 0) & (delta <= P), 0.0, NEG)

    def dilated(delta):
        n = sum(((delta >= 0) & (delta <= w) & (delta % d == 0)).astype(int) for w, d in DILATIONS)
        return np.where(n > 0, 8.0 * np.log(np.maximum(n, 1)), NEG)

    new = np.zeros((16, 385), np.float32)
    new[:, 384] = 8.0 * np.log(3.0)
    return table(window, 256), table(dilated, 1024), np.zeros((16, 129), np.float32), new


def host_inputs(i):
    fm = lambda a: np.ascontiguousarray(a)
    out = {"w": unit_list(i)}
    xs = np.concatenate([i["x_prompt"][0], i["x_sample"][:, 0]])
    out["x"] = fm(xs.T.reshape(CH, P, TOK).transpose(1, 0, 2))
    out["mem"] = fm(i["mem_prompt"][0].T.reshape(CH, P, MEM).transpose(1, 0, 2))
    g = np.stack([i["norm_mix"][0], i["norm_mix"][1], i["norm_ca"][0], i["norm_ca"][1], i["norm_mem"][0],
                  i["norm_mem"][1], i["norm_ffn"][0], i["norm_ffn"][1], i["norm_final"]])
    out["gains"] = fm(g.reshape(len(GAINS), CH, P).transpose(2, 0, 1))
    out["ident"] = np.eye(P, dtype=np.float32)
    out["token_mask"] = fm(np.repeat(np.eye(BATCH_S, dtype=np.float32), 2, axis=0))
    out["cache_conv"] = fm(i["cache_conv"][0])
    out["state_pool"] = fm(i["state_pool"][0])
    out["swa_k"] = fm(i["cache_swa_k"][0].transpose(2, 3, 0, 1).reshape(P, BATCH_S, P))
    out["swa_v"] = fm(i["cache_swa_v"][0].transpose(1, 0, 2, 3).reshape(P, BATCH_S, 1, P))
    stash = np.zeros((P, PAIRS, STASH), np.float32)
    stash[:, :, 0:3] = i["conv_w"][0].reshape(CONV_W, PAIRS, P).transpose(2, 1, 0)
    stash[:, :, 3:19] = i["cache_conv"][0].reshape(BATCH_S, 2, PAIRS, P).transpose(3, 2, 1, 0).reshape(P, PAIRS, 16)
    sinks = i["sinks"][0].reshape(2, PAIRS)
    stash[:, :, 19:21] = sinks.T[None]
    stash[0:16, :, 21] = sinks[np.arange(16) % 2]
    out["stash"] = stash
    out["mask0"], out["mask1"], out["smask0"], out["smask1"] = masks()
    out["pool_hist"] = fm(i["state_pool"][0].reshape(BATCH_S, POOL_PAD, 4, P).transpose(3, 2, 0, 1))
    out["pool_w"] = fm(i["pool_w"][0].transpose(1, 0, 2))
    rcp = 1.0 / np.minimum(np.arange(16)[None, :] + 1, np.array(POOL_WINDOWS)[:, None])
    out["pool_rcp"] = fm(np.broadcast_to(rcp.astype(np.float32), (P, 4, 16)))
    out["pool_gain"] = fm(i["pool_scale"][0].reshape(4, P).T)
    rows = np.concatenate([2048 - w + d * np.arange(P) for w, d in DILATIONS])
    dk = i["cache_dil_k"][0][:, rows].reshape(BATCH_S, 384, PAIRS, P)
    dv = i["cache_dil_v"][0][:, rows].reshape(BATCH_S, 3, P, PAIRS, P)
    out["dil_k"] = fm(dk.transpose(2, 3, 0, 1).reshape(PAIRS, P, -1))
    out["dil_v"] = fm(dv.transpose(3, 2, 0, 1, 4).reshape(PAIRS, P, -1))
    mk = i["cache_mem_k"].reshape(2, BATCH_S, MEM, CA_HEADS, 2, P)
    out["mem_cache_k"] = fm(mk.transpose(0, 3, 5, 1, 4, 2).reshape(2, CA_HEADS, P, -1))
    mv = i["cache_mem_v"].reshape(2, BATCH_S, 2, P, CA_HEADS, 2 * P)
    out["mem_cache_v"] = fm(mv.transpose(0, 4, 3, 1, 2, 5).reshape(2, CA_HEADS, P, -1))
    return out


OUTS = {"y": (P, CH, TOK), "conv_past": (BATCH_S, 512), "pool_past": (BATCH_S, 14, 512), "swa_k_out": (P, P + BATCH_S),
        "swa_v_out": (P, P + BATCH_S), "conv_out": (PAIRS, P, 10), "pool_out": (4, P, 23), "dil_k_out": (PAIRS, P, TOK),
        "dil_v_out": (PAIRS, P, TOK), "mem_k": (2, CA_HEADS, P, 2, MEM), "mem_v": (2, CA_HEADS, P, 2, MEM)}


def kernel(**inputs):
    import concourse.bacc as bacc
    from concourse.bass_utils import run_bass_kernel_spmd

    arrays = host_inputs({k: np.asarray(v) for k, v in inputs.items()})
    nc = bacc.Bacc("TRN2", target_bir_lowering=False, num_devices=1)
    dram = {n: nc.dram_tensor(f"in_{n}", a.shape, F32, kind="ExternalInput").ap() for n, a in arrays.items()}
    dram |= {n: nc.dram_tensor(f"out_{n}", s, F32, kind="ExternalOutput").ap() for n, s in OUTS.items()}
    program(nc, dram)
    r = run_bass_kernel_spmd(nc, [{f"in_{n}": a for n, a in arrays.items()}], core_ids=[0]).results[0]
    o = {n: np.asarray(r[f"out_{n}"]) for n in OUTS}

    y = o["y"].transpose(2, 1, 0).reshape(TOK, D)
    conv = o["conv_out"].transpose(2, 0, 1).reshape(10, 512)
    pooled = o["pool_out"].transpose(2, 0, 1).reshape(23, 512)
    swa = {n: o[f"swa_{n}_out"].T.reshape(P + BATCH_S, 2, HEAD) for n in "kv"}
    dil = {n: o[f"dil_{n}_out"].transpose(2, 0, 1).reshape(TOK, 8, HEAD) for n in "kv"}
    mem = {n: o[f"mem_{n}"].transpose(0, 4, 1, 3, 2).reshape(2, 1, MEM, CA_HEADS, 2 * P) for n in "kv"}
    conv_s = np.stack([o["conv_past"], conv[2:]], axis=1)
    pool_s = np.concatenate([o["pool_past"], pooled[15:, None]], axis=1)
    return (y[None, :SEQ], y[SEQ:, None],
            conv[None, None, :2], swa["k"][None, None, :P], swa["v"][None, None, :P],
            pooled[None, None, :15], dil["k"][None, None, :SEQ], dil["v"][None, None, :SEQ],
            mem["k"], mem["v"],
            conv_s[None], swa["k"][P:][None, :, None], swa["v"][P:][None, :, None],
            pool_s[None], dil["k"][SEQ:][None, :, None], dil["v"][SEQ:][None, :, None])
```

```python
from contextlib import ExitStack

import numpy as np

import concourse.bass as bass
from concourse import mybir

F32 = mybir.dt.float32
F32R = mybir.dt.float32r
ALU = mybir.AluOpType
ACT = mybir.ActivationFunctionType
AX_X = mybir.AxisListType.X

P = 128
D = 1024
SEQ = 1024
BATCH_S = 8
TOK = SEQ + BATCH_S
CH = D // P
TILE = TOK // 3
TILES = [(0, TILE), (TILE, 2 * TILE), (2 * TILE, TOK)]
MEM = 256
FFN = 2816
FFN_STEPS = FFN // 256
HEAD = 64
PAIRS = 4
CA_HEADS = 4
CONV_W = 3
POOL_WINDOWS = (2, 4, 8, 16)
POOL_PAD = 15
EPS = 1e-6
NEG = -1e30
DILATIONS = ((128, 1), (512, 4), (2048, 16))
QB = SEQ // P
GAINS = ["mix0", "mix1", "ca0", "ca1", "mem0", "mem1", "ffn0", "ffn1", "final"]
STASH = 22



JOBS = {"swa": [(qb, (0, 1)) for qb in reversed(range(QB))],
        "dil": [(qb, (h,)) for qb in range(QB - 1, 3, -1) for h in (0, 1)] + [(qb, (0, 1)) for qb in (3, 2, 1, 0)],
        "mem": [(qb, (0,)) for qb in range(QB)]}
STRIDE = {"swa": 256, "dil": 512, "mem": 256}
RING = {"swa": 3, "dil": 2, "mem": 2}



def tile_plan(name):
    three = lambda who: [(b, who) for b in range(3)]
    if name == "kv0":
        return three("dve") * 2
    if name == "att0":
        return three("dve") * 4
    if name.startswith("out") or name.startswith("caout"):
        return three("dve") * 2
    if name.startswith("cross"):
        return [(b, "dve") for b in (0, 1, 2, 0, 1, 2, 0, 1, 2, 0)]
    if name.startswith("ffn"):
        return three("dve") * 12
    if name == "pool1":
        return three("dve") * 4
    if name == "att1":
        return three("dve") * 6
    return []


def job_events(n):
    return {e: n for e in ("scored", "peaked", "biased", "exped", "inverted", "normed", "turned", "turned_in",
                           "mixed", "mixed_out")}


PER_TILE = {"squared": 1, "added": 1, "hi_ready": 1, "lo_ready": 1}
PER_NORM = {"zeroed": 1, "summed": 3, "rooted": 3, "rsqrted": 3}
MEM_NORM = {"mem_squared": 2, "mem_added": 3, "mem_summed": 1, "mem_rooted": 1, "mem_rsqrted": 1, "mem_hi": 2, "mem_lo": 2}


def phases():
    out = []
    tiles = lambda n, events=PER_TILE: {e: n * k for e, k in events.items()}
    out.append(("into_mix0", 1, 0, tiles(3 * CH)))
    for l in range(2):
        out.append((f"norm_mix{l}", 1, 0, PER_NORM))
        if l == 0:
            out.append(("kv0", 1, 2, {"v_turned": 1, "v_ready": 1}))
            out.append(("att0", PAIRS, 4, job_events(len(JOBS["swa"]) + 1) | {"q_spread": 1}))
        else:
            out.append(("pool1", 1, 4, {"delta_ready": 4, "pooled": 12, "pooled_out": 12}))
            out.append(("att1", PAIRS // 2, 6, {k: 2 * v for k, v in job_events(len(JOBS["dil"]) + 1).items()}
                        | {"q_spread": 2, "v_turned": 2, "v_ready": 2}))
        out.append((f"split{l}", 1, 0, {"hi_ready": 12, "lo_ready": 12}))
        out.append((f"out{l}", 4, 2, tiles(6)))
        out.append((f"norm_ca{l}", 1, 0, PER_NORM | MEM_NORM))
        out.append((f"cross{l}", CA_HEADS, 6, job_events(len(JOBS["mem"]) + 1) | {"q_spread": 1, "v_turned": 1, "v_ready": 1}))
        out.append((f"casplit{l}", 1, 0, {"hi_ready": 12, "lo_ready": 12}))
        out.append((f"caout{l}", 4, 2, tiles(6)))
        out.append((f"norm_ffn{l}", 1, 0, PER_NORM))
        out.append((f"ffn{l}", FFN_STEPS, 6, {"gated": 6, "hid_done": 6, "hid_hi": 6, "hid_lo": 6}))
        if l == 0:
            out.append(("into_mix1", 1, 0, tiles(3 * CH)))
        else:
            out.append(("into_final", 1, 0, {"squared": 3 * CH, "added": 3 * CH}))
    out.append(("norm_final", 1, 0, PER_NORM | {"answered": 6}))
    for i, (name, turns, units, events) in enumerate(out):
        plan = tile_plan(name)
        events = dict(events)
        if plan:
            events |= {"tile_done": len(plan), "freed_dve": len(plan)}
        if units:
            events |= {"unit_split": units, "unit_started": units}
        out[i] = (name, turns, units, events)
    return out


PHASES = phases()
CREDIT = {"unit_split": 2, "unit_started": 1, "freed_dve": 4, "peaked": 1, "exped": 1,
          "turned": 1, "mixed_out": 1, "added": 2}
N_UNITS = sum(turns * units for _, turns, units, _ in PHASES)


def at(event, phase, turn=0, k=0):
    base = CREDIT.get(event, 0)
    for name, turns, _, events in PHASES:
        per = events.get(event, 0)
        if name == phase:
            return turn * per + (base + k)
        base += turns * per
    raise KeyError(phase)


def chunk_ready(source):
    def value(t, k):
        if source.startswith("into_mix0"):
            return at("lo_ready", source, 0, CH * t + k + 1)
        if source.startswith("into"):
            return at("lo_ready", source, 0, 12 * (k // 4) + 4 * t + 4) if k % 4 == 0 else None
        if "out" in source:
            return at("lo_ready", source, 3, 3 + t + 1) if k == 0 else None
        return at("lo_ready", source, 0, 4 * t + k // 2 + 1) if k % 2 == 0 else None
    return value


def bank_wait(phase, turn, p):
    plan = tile_plan(phase)
    bank = plan[p][0]
    before = [j for j in range(p - 1, -1, -1) if plan[j][0] == bank]
    wrap = not before
    j = before[0] if before else max(i for i in range(len(plan)) if plan[i][0] == bank)
    who = plan[j][1]
    done = sum(w == who for _, w in plan[:j + 1])
    total = sum(w == who for _, w in plan)
    return f"freed_{who}", at(f"freed_{who}", phase, turn, done - (total if wrap else 0))


def freed_index(phase, p):
    plan = tile_plan(phase)
    return sum(w == plan[p][1] for _, w in plan[:p + 1])


SAMPLE_AT = {"swa": 1, "dil": 1, "mem": 0}


def scoring(kind):
    jobs = list(range(len(JOBS[kind])))
    return jobs[:SAMPLE_AT[kind]] + ["sample"] + jobs[SAMPLE_AT[kind]:]


def order_s(kind, job):
    return scoring(kind).index(job)


def pipeline(kind, emptying=False):
    n = len(JOBS[kind])
    for job in scoring(kind)[:SAMPLE_AT[kind] + 1]:
        yield "S", job
    for s in range(SAMPLE_AT[kind], n + 3):
        step = [("S", s)] if s < n else []
        step = [(w, j) for w, j in (("V", s - 3), ("T", s - 2)) if 0 <= j < n] + step if emptying else \
            step + [(w, j) for w, j in (("V", s - 3), ("T", s - 2)) if 0 <= j < n]
        yield from step
    yield "T", "sample"
    yield "V", "sample"


def order_t(job, n):
    return n if job == "sample" else job


def key_blocks(kind, job):
    qb = JOBS[kind][job][0]
    if kind == "swa":
        return max(0, qb - 1), min(2, qb + 1)
    if kind == "dil":
        return 0, qb + 1
    return 0, MEM // P


def heads_view(buf, kind, job, rows=P):
    heads, w = len(JOBS[kind][job][1]), P * key_blocks(kind, job)[1]
    if heads == 1:
        return buf[0:rows, 0:w]
    return buf[0:rows, 0:2 * STRIDE[kind]].rearrange("p (u n) -> p u n", u=2)[:, :, 0:w]


def slot_value(layer, crossing, turn, part=0):
    base, per = (0, 1) if layer == 0 else (8, 1) if crossing else (4, 2)
    return turn * (16 * per) + 16 * (base + part + 1)


def stored_before(layer, crossing, turn, part=0):
    base, per = (1, 1) if layer == 0 else (9, 1) if crossing else (5, 2)
    return turn * (16 * per) + 16 * (base + part)


KV_STORES = 16 * 13
ATT0_LOADS = 16 * 5
DVE_BASE = 1
CONV_STEPS = 6
DVE_PER_TURN = CONV_STEPS + len(JOBS["swa"]) + 1
CROSS_STEP = [DVE_BASE + PAIRS * DVE_PER_TURN + 1]
POOL_STEP = CROSS_STEP[0]
ATT1_STEP = POOL_STEP + 2 + sum(g + 5 for g in range(len(POOL_WINDOWS)))
CROSS_STEP.append(ATT1_STEP + 1)


def program(nc, dram):
    ctx = ExitStack()
    with ctx:
        cursor = [16512]

        def place(name, shape, dt=F32, offset=None):
            size = -(-int(np.prod(shape[1:])) * 4 // 32) * 32
            if offset is None:
                offset = cursor[0]
                cursor[0] += size
            assert offset + size <= 229344, (name, offset + size)
            return nc.alloc_sbuf_tensor_at(name, shape, dt, offset=offset)

        x = place("x", [P, CH, TOK])
        h_place = cursor[0]
        h_hi = place("h_hi", [P, CH, TOK], F32R)
        h_lo = place("h_lo", [P, CH, TOK], F32R)
        w_raw = place("w_raw", [P, 2, D])
        w_hi = place("w_hi", [P, 2, D], F32R)
        w_lo = place("w_lo", [P, 2, D], F32R)
        ident = place("ident", [P, P])
        gains = place("gains", [P, len(GAINS), CH])
        eps = place("eps", [P, 1])
        peak = place("peak", [P, 4])
        bias = place("bias", [P, 4])
        den = place("den", [P, 4])
        sink_exp = place("sink_exp", [P, 4])
        inv = place("inv", [P, 4])
        rs = place("rs", [P, TOK])
        token_mask = place("token_mask", [16, BATCH_S])
        sel = {kind: place(f"new_{kind}", [16, BATCH_S]) for kind in ("swa", "dil")}
        region = cursor[0]

        places = {}

        def over(*items, start=None):
            at_, out = start or region, []
            for name, shape, dt in items:
                places[name] = at_
                out.append(place(name, shape, dt, offset=at_))
                at_ += -(-int(np.prod(shape[1:])) * 4 // 32) * 32
            return out

        def over_h(*items):
            assert sum(-(-int(np.prod(shape[1:])) * 4 // 32) * 32 for _, shape, _ in items) <= 2 * CH * TOK * 4
            return over(*items, start=h_place)

        (mix0, q0, k0, v0, vnat0, vnew0, qd0, ps0, smask0, mask0, ks0, vs0, conv_u, cgate, conv_t, stash,
         cur, sink8, rs2) = over(
            ("mix0", [P, CH, TOK], F32), ("q0", [P, TOK], F32), ("k0", [P, TOK], F32), ("v0", [P, TOK], F32),
            ("vnat0", [P, QB, P], F32), ("vnew0", [BATCH_S, P], F32), ("qd0", [P, BATCH_S, 16], F32),
            ("ps0", [16, 129], F32), ("smask0", [16, 129], F32),
            ("mask0", [P, 256], F32), ("ks0", [P, BATCH_S, 128], F32), ("vs0", [P, BATCH_S, 1, P], F32),
            ("conv_u", [P, 2 + TOK], F32), ("cgate", [P, TOK], F32), ("conv_t", [P, TOK], F32),
            ("stash", [P, PAIRS, STASH], F32), ("cur", [P, STASH], F32), ("sink8", [P, 3], F32),
            ("rs2", [P, TOK], F32))
        p0, pt0 = over(("p0", [P, 3, 512], F32), ("pt0", [P, 512], F32), start=places["cgate"])
        (mix1, q1, k1, v1, vnat1, vnew1, qd1, p1, pt1, ps1, smask1, mask1, kv_slot1) = over(
            ("mix1", [P, CH, TOK], F32), ("q1", [P, TOK], F32), ("k1", [P, TOK], F32), ("v1", [P, TOK], F32),
            ("vnat1", [P, QB, P], F32), ("vnew1", [BATCH_S, P], F32), ("qd1", [P, BATCH_S, 16], F32),
            ("p1", [P, 2, 1024], F32), ("pt1", [P, 1024], F32), ("ps1", [16, 385], F32), ("smask1", [16, 385], F32),
            ("mask1", [P, 1024], F32), ("kv_slot1", [P, BATCH_S * 384], F32))
        (_, pool_u, pool_a, pool_b, pool_d, pool_hist, pool_w, pool_rcp, pool_gain, pool_s) = over(
            ("mix1_", [P, CH, TOK], F32), ("pool_u", [P, POOL_PAD + TOK], F32), ("pool_a", [P, POOL_PAD + SEQ], F32),
            ("pool_b", [P, POOL_PAD + SEQ], F32), ("pool_d", [P, 2, TOK], F32),
            ("pool_hist", [P, 4, BATCH_S, POOL_PAD], F32), ("pool_w", [P, 4, P], F32), ("pool_rcp", [P, 4, 16], F32),
            ("pool_gain", [P, 4], F32), ("pool_s", [P, 2, BATCH_S], F32))
        g_hi, g_lo, mem_hi, mem_lo, ptc, qdc = over(
            ("g_hi", [P, CH, TOK], F32R), ("g_lo", [P, CH, TOK], F32R), ("mem_hi", [P, CH, MEM], F32R),
            ("mem_lo", [P, CH, MEM], F32R), ("ptc", [P, 256], F32), ("qdc", [P, 2, BATCH_S, 8], F32))
        mem_half = over(("mem_half", [P, MEM], F32))[0]
        mem_raw = over(("mem_raw", [P, CH, MEM], F32), start=places["mem_lo"])[0]
        mem_sum = over(("mem_sum", [P, MEM], F32), start=places["ptc"])[0]
        ones = over(("ones", [P, P], F32), start=places["qdc"])[0]
        mixc, kv_slotc, qc, kc, vnatc, p_c, psc, mem_rs = over_h(
            ("mixc", [P, CH, TOK], F32), ("kv_slotc", [P, BATCH_S * 512], F32), ("qc", [P, 2, TOK], F32),
            ("kc", [P, 2, MEM], F32), ("vnatc", [P, 2, MEM], F32), ("p_c", [P, 2, 256], F32), ("psc", [8, 256], F32),
            ("mem_rs", [P, MEM], F32))
        vc = over(("vc", [P, 2, MEM], F32), start=places["p_c"])[0]
        answer = over(("answer", [P, CH, TOK], F32))[0]
        hid_hi, hid_lo, gate, hid, sq_all = over(
            ("hid_hi", [P, 2, TOK], F32R), ("hid_lo", [P, 2, TOK], F32R), ("gate", [P, TOK], F32), ("hid", [P, TOK], F32),
            ("sq_all", [P, CH, TOK], F32))

        lin3 = ctx.enter_context(nc.psum_tensor("linear", [P, 3 * 512], F32))
        lin = [lin3[:, 512 * i:512 * i + 512] for i in range(3)]
        ps_s = ctx.enter_context(nc.psum_tensor("ps_scores", [P, 1024], F32))
        ps_t = ctx.enter_context(nc.psum_tensor("ps_turned", [P, 1024], F32))
        ps_o = ctx.enter_context(nc.psum_tensor("ps_mixed", [P, 512], F32))
        score_banks = [ps_s[:, :], lin3[:, 0:1024]]
        sq_banks = [ps_t[:, 512:1024], ps_o[:, :]]
        sum_banks = [ps_s[:, 0:512], ps_s[:, 512:1024], ps_t[:, 0:512]]

        names = sorted({e for _, _, _, ev in PHASES for e in ev})
        sem = {n: ctx.enter_context(nc.semaphore(n)) for n in names}
        gate_sem = {n: ctx.enter_context(nc.semaphore(f"passed_{n}")) for n in ("pe", "act", "dve", "pool")}
        dve_step = ctx.enter_context(nc.semaphore("dve_step"))
        landed = [ctx.enter_context(nc.semaphore(f"unit_landed{i}")) for i in range(2)]
        loads = {n: ctx.enter_context(nc.semaphore(f"load_{n}")) for n in
                 ("x00", "x01", "x1", "x2", "consts", "att0", "pool1", "att1", "mem0", "mem1", "k_slot", "v_slot", "mask1")}
        consts_set = ctx.enter_context(nc.semaphore("consts_set"))
        pool_hi = ctx.enter_context(nc.semaphore("unit_hi"))
        stored = {n: ctx.enter_context(nc.semaphore(f"stored_{n}")) for n in ("k", "v", "u", "y", "past")}
        block = ctx.enter_context(nc.Block())

        def flat(ap):
            return ap if len(ap.shape) == 2 else ap.rearrange("p a n -> p (a n)")


        INTO = {}
        for l in range(2):
            INTO |= {f"out{l}": (GAINS.index(f"ca{l}"), g_hi, g_lo), f"caout{l}": (GAINS.index(f"ffn{l}"), h_hi, h_lo),
                     f"into_mix{l}": (GAINS.index(f"mix{l}"), h_hi, h_lo)}
        INTO["into_final"] = (GAINS.index("final"), None, None)

        @block.sync
        def _(sp):
            sp.dma_start(gains[:], dram["gains"]).then_inc(loads["consts"], 16)
            sp.dma_start(ident[:], dram["ident"]).then_inc(loads["consts"], 16)
            sp.dma_start(token_mask[:], dram["token_mask"]).then_inc(loads["consts"], 16)
            for half in range(2):
                c = slice(4 * half, 4 * half + 4)
                sp.dma_start(x[:, c, 0:TILE], dram["x"][:, c, 0:TILE]).then_inc(loads[f"x0{half}"], 16)
            with sp.Fori(0, N_UNITS // 2) as i:
                for s in range(2):
                    sp.wait_ge(sem["unit_split"], 2 * i + (s + 1))
                    sp.dma_start(w_raw[:, s, :], dram["w"][bass.ds(2 * i + s, 1)].rearrange("a p n -> p (a n)")
                                 ).then_inc(landed[s], 16)
            sp.wait_ge(stored["past"], 32)

        @block.gpsimd
        def _(pool):
            pool.memset(eps[:], EPS).then_inc(consts_set, 1)
            for name, n in CREDIT.items():
                if n:
                    pool.sem_inc(sem[name], n)
            pool.sem_inc(stored["u"], 16)
            with pool.Fori(0, N_UNITS // 2) as i:
                for s in range(2):
                    pool.wait_ge(landed[s], 16 * i + 16)
                    pool.wait_ge(sem["unit_started"], 2 * i + (s + 1))
                    pool.sem_inc(gate_sem["pool"], 1)
                    pool.tensor_scalar(w_hi[:, s, :], w_raw[:, s, :], 1.0, 0.0, ALU.mult, ALU.add).then_inc(pool_hi, 1)
                    pool.wait_ge(pool_hi, 2 * i + (s + 1))
                    pool.tensor_tensor(w_lo[:, s, :], w_raw[:, s, :], w_hi[:, s, :].bitcast(F32), ALU.subtract
                                       ).then_inc(sem["unit_split"], 1)

        @block.tensor
        def _(pe):
            def past_waits():
                pe.sem_inc(gate_sem["pe"], 1)

            def sums(t, value):
                a, b = TILES[t]
                pe.wait_ge(sem["added"], value)
                pe.matmul(sum_banks[t][:, 0:b - a], ones[:], rs[:, a:b], start=True, stop=True).then_inc(sem["summed"], 1)

            def sums_after(phase):
                for t in range(3):
                    sums(t, at("added", phase, 3, 3 + t + 1))

            def enter(phase):
                pe.wait_ge(sem["freed_dve"], at("freed_dve", phase))

            def passes(out, slot, terms, unit_first=False, ready=None):
                n = len(terms)
                for k, (cols, hi, lo) in enumerate(terms):
                    if ready and ready(k) is not None:
                        pe.wait_ge(sem["lo_ready"], ready(k))
                    for j, (w, a) in enumerate(((w_hi, hi), (w_hi, lo), (w_lo, hi))):
                        mm = pe.matmul(out, w[:, slot, cols], a, start=(k == 0 and j == 0), stop=(k == n - 1 and j == 2))
                        if unit_first and k == 0 and j == 0:
                            mm.then_inc(sem["unit_started"], 1)
                mm.then_inc(sem["tile_done"], 1)

            def unit(phase, turn, u, p, tiles, hi, lo, ready=None, after=None):
                pe.wait_ge(sem["unit_split"], at("unit_split", phase, turn, u + 1))
                for t, (a, b) in enumerate(tiles):
                    bank = tile_plan(phase)[p][0]
                    name, value = bank_wait(phase, turn, p)
                    pe.wait_ge(sem[name], value)
                    passes(lin[bank][:, 0:b - a], u % 2,
                           [(slice(P * k, P * k + P), hi[:, k, a:b], lo[:, k, a:b]) for k in range(CH)],
                           unit_first=(t == 0), ready=ready and (lambda k: ready(t, k)))
                    if after:
                        after(t)
                    p += 1
                return p

            def turn_values(phase, turn, k, v, n, new):
                pe.wait_ge(sem[n[0]], n[1])
                pe.wait_ge(sem["mixed_out"], at("mixed_out", *new))
                for b in range(QB):
                    pe.transpose(ps_t[:, P * b:P * b + P], v[:, P * b:P * b + P], ident[:])
                pe.transpose(ps_o[0:BATCH_S, 0:P], v[:, SEQ:TOK], ident[:]).then_inc(sem["v_turned"], 1)

            def attention(phase, turn, kind, q, k, vnat, vnew, qd, p, pt, ps, ks, vs, emptied, part=0, slots=None, turn_v=None):
                n = len(JOBS[kind])
                jobs_before = part * (n + 1)
                freed = "exped" if kind == "mem" else "peaked"
                for what, job in pipeline(kind):
                    s, t = jobs_before + order_s(kind, job), jobs_before + order_t(job, n)
                    if what == "S":
                        pe.wait_ge(sem[freed], at(freed, phase, turn, jobs_before + max(order_s(kind, job) - 1, 0)))
                        if order_s(kind, job) == 1:
                            for name, value in emptied:
                                pe.wait_ge(sem[name], value)
                        sc = score_banks[order_s(kind, job) % 2]
                        if job == "sample":
                            pe.wait_ge(sem["q_spread"], at("q_spread", phase, turn, part + 1))
                            if slots is not None:
                                pe.wait_ge(loads["k_slot"], slots)
                            past_waits()
                            if kind == "mem":
                                todo = [(sc[0:8, 0:256], qd[:, c, b, :], ks[:, b, c, :])
                                        for b in range(BATCH_S) for c in range(2)]
                            else:
                                nk = ks.shape[2]
                                todo = [(sc[0:16, 0:nk], qd[:, b, :], ks[:, b, :]) for b in range(BATCH_S)]
                                todo += [(sc[0:16, nk:nk + 1], qd[:, b, :], k[:, SEQ + b:SEQ + b + 1])
                                         for b in range(BATCH_S)]
                            for j, (o, w, a) in enumerate(todo):
                                mm = pe.matmul(o, w, a, start=(j == 0), stop=(j == len(todo) - 1), skip_group_check=True)
                        elif kind == "mem":
                            for c in range(2):
                                mm = pe.matmul(sc[:, 0:MEM], q[:, c, P * job:P * job + P], k[:, c, :],
                                               start=(c == 0), stop=(c == 1))
                        else:
                            kb, nb = key_blocks(kind, job)
                            qb, heads = JOBS[kind][job]
                            for u, h in enumerate(heads):
                                r, at_ = HEAD * h, 512 * u
                                for o in range(0, nb * P, 512):
                                    w = min(512, nb * P - o)
                                    mm = pe.matmul(sc[:, at_ + o:at_ + o + w], q[r:r + HEAD, P * qb:P * qb + P],
                                                   k[r:r + HEAD, P * kb + o:P * kb + o + w], start=True, stop=True)
                        mm.then_inc(sem["scored"], 1)
                        if job == "sample" and turn_v:
                            turn_v()
                    elif what == "T":
                        if job == 0:
                            pe.wait_ge(sem["v_ready"], at("v_ready", "kv0" if kind == "swa" else phase,
                                                          0 if kind == "swa" else turn, 1 if kind == "swa" else part + 1))
                        pe.wait_ge(sem["normed"], at("normed", phase, turn, s + 1))
                        past_waits()
                        if job == "sample":
                            rows = 8 if kind == "mem" else 16
                            nkb = 2 if kind == "mem" else ks.shape[2] // P
                            for b in range(nkb):
                                mm = pe.transpose(ps_t[:, rows * b:rows * b + rows], ps[:, P * b:P * b + P],
                                                  ident[0:rows, 0:rows])
                            if kind != "mem":
                                mm = pe.transpose(ps_t[0:BATCH_S, 512:528], sel[kind][:], ident[0:rows, 0:rows])
                        else:
                            for u in range(len(JOBS[kind][job][1])):
                                for b in range(key_blocks(kind, job)[1]):
                                    o = STRIDE[kind] * u + P * b
                                    mm = pe.transpose(ps_t[:, o:o + P], p[:, job % RING[kind], o:o + P], ident[:])
                        mm.then_inc(sem["turned"], 1)
                    else:
                        pe.wait_ge(sem["turned_in"], at("turned_in", phase, turn, t + 1))
                        pe.wait_ge(sem["mixed_out"], at("mixed_out", phase, turn, t))
                        if job == "sample":
                            if slots is not None:
                                pe.wait_ge(loads["v_slot"], slots)
                            past_waits()
                            if kind == "mem":
                                todo = [(ps_o[:, 8 * c + b:8 * c + b + 1], vs[:, b, m, P * c:P * c + P],
                                         pt[:, 8 * m + b:8 * m + b + 1])
                                        for b in range(BATCH_S) for c in range(2) for m in range(2)]
                            else:
                                nkb = ks.shape[2] // P
                                todo = [(ps_o[:, 0:16], vnew[:, :], pt[0:BATCH_S, 16 * nkb:16 * nkb + 16])]
                                todo += [(ps_o[:, 2 * b:2 * b + 2], vs[:, b, m, :],
                                          pt[:, 16 * m + 2 * b:16 * m + 2 * b + 2])
                                         for b in range(BATCH_S) for m in range(nkb)]
                            for j, (o, w, a) in enumerate(todo):
                                mm = pe.matmul(o, w, a, start=(j == 0), stop=(j == len(todo) - 1), skip_group_check=True)
                        elif kind == "mem":
                            for c in range(2):
                                for m in range(2):
                                    mm = pe.matmul(ps_o[:, P * c:P * c + P], vnat[:, m, P * c:P * c + P],
                                                   pt[:, P * m:P * m + P], start=(m == 0), stop=(m == 1))
                        else:
                            kb, nb = key_blocks(kind, job)
                            for u, h in enumerate(JOBS[kind][job][1]):
                                r = HEAD * h
                                for m in range(nb):
                                    o = STRIDE[kind] * u + P * m
                                    mm = pe.matmul(ps_o[r:r + HEAD, 0:P], vnat[:, kb + m, r:r + HEAD],
                                                   pt[:, o:o + P], start=(m == 0), stop=(m == nb - 1))
                        mm.then_inc(sem["mixed"], 1)

            def linear_out(phase, hi, lo, source):
                enter(phase)
                with pe.Fori(0, 4) as i:
                    p = 0
                    for u in range(2):
                        p = unit(phase, i, u, p, TILES, hi, lo, chunk_ready(source) if u == 0 else None)

            def cross(l):
                ph = f"cross{l}"
                sums_after(f"out{l}")
                pe.wait_ge(sem["mem_added"], at("mem_added", f"norm_ca{l}", 0, 3))
                pe.matmul(ps_o[:, 0:MEM], ones[:], mem_sum[:], start=True, stop=True).then_inc(sem["mem_summed"], 1)
                enter(ph)
                pe.wait_ge(sem["mem_lo"], at("mem_lo", f"norm_ca{l}", 0, 2))
                with pe.Fori(0, CA_HEADS) as i:
                    p = unit(ph, i, 0, 0, [(0, MEM)], mem_hi, mem_lo)
                    p = unit(ph, i, 1, p, TILES, g_hi, g_lo, chunk_ready(f"out{l}"))
                    for u in (2, 3):
                        p = unit(ph, i, u, p, [(0, MEM)], mem_hi, mem_lo)
                    p = unit(ph, i, 4, p, TILES, g_hi, g_lo)
                    p = unit(ph, i, 5, p, [(0, MEM)], mem_hi, mem_lo)

                    def turn_mem_values():
                        pe.wait_ge(sem["freed_dve"], at("freed_dve", ph, i, 10))
                        for c in range(2):
                            for m in range(2):
                                mm = pe.transpose(ps_t[:, MEM * m + P * c:MEM * m + P * c + P], vc[:, c, P * m:P * m + P],
                                                  ident[:])
                        mm.then_inc(sem["v_turned"], 1)

                    pe.wait_ge(sem["freed_dve"], at("freed_dve", ph, i, 9))
                    attention(ph, i, "mem", qc, kc, vnatc, None, qdc, p_c, ptc, psc,
                              kv_slotc[:, :].rearrange("p (b c n) -> p b c n", b=BATCH_S, c=2),
                              kv_slotc[:, :].rearrange("p (b m d) -> p b m d", b=BATCH_S, m=2),
                              [("freed_dve", at("freed_dve", ph, i, 10))], turn_v=turn_mem_values,
                              slots=slot_value(l, 1, i))

            def ffn(l):
                ph = f"ffn{l}"
                sums_after(f"caout{l}")
                enter(ph)

                def step(i, last):
                    p = 0
                    for u in range(4):
                        p = unit(ph, i, u, p, TILES, h_hi, h_lo, chunk_ready(f"caout{l}") if u == 0 else None)
                    for u in range(4, 6):
                        pe.wait_ge(sem["unit_split"], at("unit_split", ph, i, u + 1))
                        for t, (a, b) in enumerate(TILES):
                            pe.wait_ge(sem["hid_lo"], at("hid_lo", ph, i, 3 + t + 1))
                            for n in range(4):
                                name, value = bank_wait(ph, i, p)
                                pe.wait_ge(sem[name], value)
                                passes(lin[tile_plan(ph)[p][0]][:, 0:b - a], u % 2,
                                       [(slice(512 * k + P * n, 512 * k + P * n + P), hid_hi[:, k, a:b], hid_lo[:, k, a:b])
                                        for k in range(2)], unit_first=(t == 0 and n == 0))
                                p += 1
                            if last and l == 1 and u == 5 and t:
                                sums(t - 1, at("added", "into_final", 0, 12 + 4 * t))

                with pe.Fori(0, FFN_STEPS - 1) as i:
                    step(i, False)
                step(FFN_STEPS - 1, True)

            pe.wait_ge(loads["consts"], 48)
            enter("kv0")
            p = unit("kv0", 0, 0, 0, TILES, h_hi, h_lo, chunk_ready("into_mix0"),
                     after=lambda t: sums(t, at("added", "into_mix0", 0, CH * (t + 1))))
            p = unit("kv0", 0, 1, p, TILES, h_hi, h_lo)
            turn_values("kv0", 0, k0, v0, ("freed_dve", at("freed_dve", "kv0", 0, 6)), ("att0", 0, 0))
            enter("att0")
            pe.wait_ge(loads["att0"], ATT0_LOADS)
            with pe.Fori(0, PAIRS) as i:
                p = 0
                for u in range(4):
                    p = unit("att0", i, u, p, TILES, h_hi, h_lo)
                pe.wait_ge(sem["freed_dve"], at("freed_dve", "att0", i, 3))
                attention("att0", i, "swa", q0, k0, vnat0, vnew0, qd0, p0, pt0, ps0, ks0, vs0,
                          [("freed_dve", at("freed_dve", "att0", i, 12))])
            linear_out("out0", h_hi, h_lo, "split0")
            cross(0)
            linear_out("caout0", g_hi, g_lo, "casplit0")
            ffn(0)
            enter("pool1")

            def pool_map(g):
                pe.wait_ge(sem["delta_ready"], at("delta_ready", "pool1", 0, g + 1))
                for t, (a, b) in enumerate(TILES):
                    if g:
                        pe.wait_ge(sem["pooled_out"], at("pooled_out", "pool1", 0, 3 * (g - 1) + t + 1))
                    pe.matmul(sum_banks[t][:, 0:b - a], pool_w[:, g, :], pool_d[:, g % 2, a:b], start=True, stop=True
                              ).then_inc(sem["pooled"], 1)

            p = 0
            for g in range(4):
                p = unit("pool1", 0, g, p, TILES, h_hi, h_lo, chunk_ready("into_mix1") if g == 0 else None,
                         after=(lambda t: sums(t, at("added", "into_mix1", 0, CH * (t + 1)))) if g == 0 else None)
                if g == 1:
                    pe.wait_ge(loads["pool1"], 64)
                if g:
                    pool_map(g - 1)
            pool_map(3)
            enter("att1")
            pe.wait_ge(sem["pooled_out"], at("pooled_out", "pool1", 0, 12))
            with pe.Fori(0, PAIRS // 2) as i:
                p = 0
                for part in range(2):
                    for u in range(3):
                        p = unit("att1", i, 3 * part + u, p, TILES, h_hi, h_lo)
                    pe.wait_ge(sem["freed_dve"], at("freed_dve", "att1", i, 9 * part + 6))
                    attention("att1", i, "dil", q1, k1, vnat1, vnew1, qd1, p1, pt1, ps1,
                              kv_slot1[:, :].rearrange("p (b n) -> p b n", b=BATCH_S),
                              kv_slot1[:, :].rearrange("p (b m d) -> p b m d", b=BATCH_S, m=3),
                              [("freed_dve", at("freed_dve", "att1", i, 9 * part + 9))], part=part,
                              turn_v=lambda: turn_values("att1", i, k1, v1, ("freed_dve", at("freed_dve", "att1", i, 9 * part + 9)),
                                                         ("att1", i, part * (len(JOBS["dil"]) + 1))),
                              slots=slot_value(1, 0, i, part))
            linear_out("out1", h_hi, h_lo, "split1")
            cross(1)
            linear_out("caout1", g_hi, g_lo, "casplit1")
            ffn(1)
            sums(2, at("added", "into_final", 0, 24))

        @block.scalar
        def _(act):
            def past_waits():
                act.sem_inc(gate_sem["act"], 1)

            def copy(out, in_, **kw):
                return act.activation(out, in_, ACT.Copy, **kw)

            def roots(name):
                for t, (a, b) in enumerate(TILES):
                    act.wait_ge(sem["summed"], at("summed", name, 0, t + 1))
                    act.activation(rs[:, a:b], sum_banks[t][:, 0:b - a], ACT.Sqrt, bias=eps[:, 0:1], scale=1.0 / D
                                   ).then_inc(sem["rooted"], 1)

            def follow(source, turn, k, n, a, b, sq=None):
                g, hi, _ = INTO[source]
                xs = x[:, n, a:b]
                gain = gains[:, g, n]
                if sq is None:
                    act.wait_ge(sem["added"], at("added", source, turn, k - 1))
                past_waits()
                act.activation(sq_banks[k % 2][:, 0:b - a] if sq is None else sq, flat(xs), ACT.Square
                               ).then_inc(sem["squared"], 1)
                if hi is not None:
                    copy(flat(hi[:, n, a:b]), flat(xs), scale=gain).then_inc(sem["hi_ready"], 1)

            def follow_out(phase):
                with act.Fori(0, 4) as i:
                    for p in range(6):
                        act.wait_ge(sem["freed_dve"], at("freed_dve", phase, i, p + 1))
                        follow(phase, i, p, bass.ds(2 * i + p // 3, 1), *TILES[p % 3])

            def split(phase, mix, before, hi):
                act.wait_ge(sem["mixed_out"], at("mixed_out", phase))
                act.wait_ge(sem["freed_dve"], at("freed_dve", phase))
                act.wait_ge(sem["tile_done"], at("tile_done", phase))
                for t, (a, b) in enumerate(TILES):
                    for q in range(4):
                        c = slice(2 * q, 2 * q + 2)
                        copy(hi[:, c, a:b], mix[:, c, a:b]).then_inc(sem["hi_ready"], 1)
                act.wait_ge(sem["lo_ready"], at("lo_ready", phase, 0, 12))

            def values_in(vnat, vnew, phase, turn, k):
                act.wait_ge(sem["v_turned"], at("v_turned", phase, turn, k + 1))
                copy(vnat[:, :, :], ps_t[:, 0:1024].rearrange("p (b d) -> p b d", b=QB))
                copy(vnew[:, :], ps_o[0:BATCH_S, 0:P]).then_inc(sem["v_ready"], 1)

            def attention(phase, turn, kind, mix, chunk, p, pt, ps, part=0, values=None, turned_v=None):
                n = len(JOBS[kind])
                before = part * (n + 1)
                scale = 1.0 / 16.0 if kind == "mem" else 1.0 / 8.0
                nkb = {"swa": 1, "dil": 3, "mem": 2}[kind]
                rows = 8 if kind == "mem" else 16
                for what, job in pipeline(kind, emptying=True):
                    s, t = before + order_s(kind, job), before + order_t(job, n)
                    o = order_s(kind, job) % 2
                    if what == "S":
                        act.wait_ge(sem["biased"], at("biased", phase, turn, s + 1))
                        if kind == "mem" and job != "sample" and job >= 2:
                            act.wait_ge(sem["turned"], at("turned", phase, turn, before + job - 1))
                        heads = (0,) if job == "sample" else JOBS[kind][job][1]
                        m = rows if job == "sample" else P
                        for u, h in enumerate(heads):
                            c = 2 * o + u
                            if job == "sample":
                                dst = ps[:, :]
                            else:
                                at_ = STRIDE[kind] * u
                                dst = p[:, job % RING[kind], at_:at_ + P * key_blocks(kind, job)[1]]
                            src = score_banks[o][0:m, 0:MEM] if kind == "mem" else dst
                            if kind == "swa":
                                sc = 2 if job == "sample" else h
                                act.activation(sink_exp[0:m, c:c + 1], sink8[0:m, sc:sc + 1], ACT.Exp, scale=scale,
                                               bias=bias[0:m, c:c + 1])
                            mm = act.activation(dst, src, ACT.Exp, scale=scale, bias=bias[0:m, c:c + 1],
                                                accum_out=den[0:m, c:c + 1])
                        mm.then_inc(sem["exped"], 1)
                        if job == "sample" and values is not None:
                            slot, src_v = values
                            act.dma_start(slot, src_v).then_inc(loads["v_slot"], 16)
                        if job == "sample" and turned_v:
                            turned_v()
                    elif what == "T":
                        act.wait_ge(sem["turned"], at("turned", phase, turn, t + 1))
                        if job == "sample":
                            mm = copy(pt[:, 0:rows * nkb], ps_t[:, 0:rows * nkb])
                            if kind != "mem":
                                mm = copy(pt[0:BATCH_S, 16 * nkb:16 * nkb + 16], ps_t[0:BATCH_S, 512:528])
                        else:
                            mm = copy(heads_view(pt, kind, job), heads_view(ps_t, kind, job))
                        mm.then_inc(sem["turned_in"], 1)
                    else:
                        act.wait_ge(sem["mixed"], at("mixed", phase, turn, t + 1))
                        past_waits()
                        if kind == "mem":
                            a, w = (SEQ, 8) if job == "sample" else (P * job, P)
                            mm = copy(mix[:, bass.ds(chunk, 2), a:a + w],
                                      ps_o[:, 0:2 * w].rearrange("p (c n) -> p c n", c=2))
                        elif job == "sample":
                            copy(mix[0:HEAD, bass.ds(chunk, 1), SEQ:TOK], ps_o[0:HEAD, 0:16:2].rearrange("p (a n) -> p a n", a=1))
                            mm = copy(mix[HEAD:P, bass.ds(chunk, 1), SEQ:TOK],
                                      ps_o[HEAD:P, 1:16:2].rearrange("p (a n) -> p a n", a=1))
                        else:
                            qb, heads = JOBS[kind][job]
                            r, r_end = HEAD * heads[0], HEAD * (heads[-1] + 1)
                            mm = copy(mix[r:r_end, bass.ds(chunk, 1), P * qb:P * qb + P],
                                      ps_o[r:r_end, 0:P].rearrange("p (a n) -> p a n", a=1))
                        mm.then_inc(sem["mixed_out"], 1)

            def cross(l):
                ph = f"cross{l}"
                with act.Fori(0, CA_HEADS) as i:
                    act.wait_ge(sem["tile_done"], at("tile_done", ph, i, 1))
                    act.dma_start(kv_slotc[:, :], dram["mem_cache_k"][l, bass.ds(i, 1)].rearrange("a p n -> p (a n)")
                                  ).then_inc(loads["k_slot"], 16)
                    act.wait_ge(sem["freed_dve"], at("freed_dve", ph, i, 5))
                    act.dma_start(dram["mem_k"][l, bass.ds(i, 1)].rearrange("a p c n -> p (a c) n"), kc[:]).then_inc(stored["k"], 16)
                    act.wait_ge(sem["freed_dve"], at("freed_dve", ph, i, 10))
                    act.dma_start(dram["mem_v"][l, bass.ds(i, 1)].rearrange("a p c n -> p (a c) n"), vc[:]).then_inc(stored["v"], 16)

                    def values_turned():
                        act.wait_ge(sem["v_turned"], at("v_turned", ph, i, 1))
                        copy(vnatc[:, :, :], ps_t[:, 0:512].rearrange("p (m d) -> p m d", m=2)).then_inc(sem["v_ready"], 1)
                        act.wait_ge(stored["v"], stored_before(l, 1, i + 1))

                    attention(ph, i, "mem", mixc, 2 * i, p_c, ptc, psc,
                              values=(kv_slotc[:, :], dram["mem_cache_v"][l, bass.ds(i, 1)].rearrange("a p n -> p (a n)")),
                              turned_v=values_turned)
                split(f"casplit{l}", mixc, ph, g_hi)
                follow_out(f"caout{l}")
                roots(f"norm_ffn{l}")

            def ffn(l):
                ph = f"ffn{l}"

                def step(i):
                    for c in range(2):
                        for t, (a, b) in enumerate(TILES):
                            act.wait_ge(sem["freed_dve"], at("freed_dve", ph, i, 6 * c + t + 1))
                            act.activation(gate[:, a:b], gate[:, a:b], ACT.Silu).then_inc(sem["gated"], 1)
                        for t, (a, b) in enumerate(TILES):
                            act.wait_ge(sem["hid_done"], at("hid_done", ph, i, 3 * c + t + 1))
                            copy(hid_hi[:, c, a:b], hid[:, a:b]).then_inc(sem["hid_hi"], 1)

                with act.Fori(0, FFN_STEPS - 1) as i:
                    step(i)
                step(FFN_STEPS - 1)
                source = ("into_mix1", "into_final")[l]
                act.wait_ge(sem["tile_done"], at("tile_done", ph, FFN_STEPS - 1, 12))
                for half in range(2):
                    for t, (a, b) in enumerate(TILES):
                        for n in range(4):
                            k = 12 * half + 4 * t + n
                            act.wait_ge(sem["freed_dve"], at("freed_dve", ph, FFN_STEPS - 1, 12 + k + 1))
                            follow(source, 0, k, slice(4 * half + n, 4 * half + n + 1), a, b, sq=sq_all[:, 4 * half + n, a:b])
                roots(("norm_mix1", "norm_final")[l])

            act.wait_ge(consts_set, 1)
            act.wait_ge(loads["consts"], 48)
            for t, (a, b) in enumerate(TILES):
                for n in range(CH):
                    if t == 0 and n % 4 == 0:
                        act.wait_ge(loads[f"x0{n // 4}"], 16)
                    elif n == 0:
                        act.wait_ge(loads[f"x{t}"], 16)
                    follow("into_mix0", 0, CH * t + n, slice(n, n + 1), a, b)
                    if t == 0 and n == 4:
                        for u in (1, 2):
                            c, d = TILES[u]
                            act.dma_start(x[:, :, c:d], dram["x"][:, :, c:d]).then_inc(loads[f"x{u}"], 16)
                if t == 1:
                    for dst, name in ((ks0, "swa_k"), (vs0, "swa_v"), (stash, "stash"), (mask0, "mask0"), (smask0, "smask0")):
                        act.dma_start(dst[:], dram[name]).then_inc(loads["att0"], 16)
            act.dma_start(dram["conv_past"], dram["cache_conv"][:, 1, :]).then_inc(stored["past"], 16)
            act.dma_start(dram["pool_past"], dram["state_pool"][:, 1:, :]).then_inc(stored["past"], 16)
            roots("norm_mix0")
            act.wait_ge(sem["freed_dve"], at("freed_dve", "kv0", 0, 6))
            act.dma_start(dram["swa_k_out"], k0[:, SEQ - P:TOK]).then_inc(stored["k"], 16)
            act.dma_start(dram["swa_v_out"], v0[:, SEQ - P:TOK]).then_inc(stored["v"], 16)
            values_in(vnat0, vnew0, "kv0", 0, 0)
            with act.Fori(0, PAIRS) as i:
                act.wait_ge(sem["freed_dve"], at("freed_dve", "att0", i, 9))
                act.dma_start(dram["conv_out"][bass.ds(i, 1)].rearrange("a p n -> p (a n)"), conv_u[:, SEQ:2 + TOK]
                              ).then_inc(stored["u"], 16)
                attention("att0", i, "swa", mix0, i + 4, p0, pt0, ps0)
            def out_and_memory(l, mix):
                ph = f"norm_ca{l}"
                act.wait_ge(sem["mixed_out"], at("mixed_out", f"split{l}"))
                act.dma_start(mem_raw[:], dram["mem"]).then_inc(loads[f"mem{l}"], 16)
                split(f"split{l}", mix, f"att{l}", h_hi)
                act.wait_ge(loads[f"mem{l}"], 16)
                g = GAINS.index(f"mem{l}")

                def mem_squares(half):
                    act.activation(ps_s[:, :].rearrange("p (c n) -> p c n", c=4), mem_raw[:, 4 * half:4 * half + 4, :],
                                   ACT.Square).then_inc(sem["mem_squared"], 1)

                mem_squares(0)
                for half in range(2):
                    for c in range(4 * half, 4 * half + 4):
                        mm = copy(mem_hi[:, c, :], mem_raw[:, c, :], scale=gains[:, g, c:c + 1])
                    mm.then_inc(sem["mem_hi"], 1)
                    if half == 0:
                        act.wait_ge(sem["mem_added"], at("mem_added", ph, 0, 1))
                        mem_squares(1)
                act.wait_ge(sem["mem_added"], at("mem_added", ph, 0, 3))
                follow_out(f"out{l}")
                roots(ph)
                act.wait_ge(sem["mem_summed"], at("mem_summed", ph, 0, 1))
                act.activation(mem_rs[:], ps_o[:, 0:MEM], ACT.Sqrt, bias=eps[:, 0:1], scale=1.0 / D).then_inc(sem["mem_rooted"], 1)

            out_and_memory(0, mix0)
            cross(0)
            ffn(0)
            act.wait_ge(sem["added"], at("added", "into_mix1", 0, 24))
            for dst, name in ((pool_hist, "pool_hist"), (pool_w, "pool_w"), (pool_rcp, "pool_rcp"), (pool_gain, "pool_gain")):
                act.dma_start(dst[:], dram[name]).then_inc(loads["pool1"], 16)
            act.wait_ge(loads["pool1"], 64)

            def pool_out(g):
                for t, (a, b) in enumerate(TILES):
                    act.wait_ge(sem["pooled"], at("pooled", "pool1", 0, 3 * g + t + 1))
                    copy(mix1[:, g, a:b], sum_banks[t][:, 0:TILE], scale=pool_gain[:, g:g + 1]
                         ).then_inc(sem["pooled_out"], 1)

            for g in range(4):
                act.wait_ge(sem["freed_dve"], at("freed_dve", "pool1", 0, 3 * g + 3))
                act.dma_start(dram["pool_out"][g], pool_u[:, SEQ:POOL_PAD + TOK]).then_inc(stored["u"], 16)
                if g:
                    pool_out(g - 1)
            pool_out(3)
            act.wait_ge(stored["u"], 16 * (PAIRS + 5))
            act.wait_ge(sem["pooled_out"], at("pooled_out", "pool1", 0, 12))
            act.dma_start(mask1[:], dram["mask1"]).then_inc(loads["att1"], 16)
            act.dma_start(smask1[:], dram["smask1"]).then_inc(loads["att1"], 16)
            with act.Fori(0, PAIRS // 2) as i:
                for part in range(2):
                    act.dma_start(kv_slot1[:, :], dram["dil_k"][bass.ds(2 * i + part, 1)].rearrange("a p n -> p (a n)")
                                  ).then_inc(loads["k_slot"], 16)
                    act.wait_ge(sem["freed_dve"], at("freed_dve", "att1", i, 9 * part + 9))
                    act.dma_start(dram["dil_k_out"][bass.ds(2 * i + part, 1)].rearrange("a p n -> p (a n)"), k1[:, :]
                                  ).then_inc(stored["k"], 16)
                    act.dma_start(dram["dil_v_out"][bass.ds(2 * i + part, 1)].rearrange("a p n -> p (a n)"), v1[:, :]
                                  ).then_inc(stored["v"], 16)
                    attention("att1", i, "dil", mix1, 2 * i + (4 + part), p1, pt1, ps1, part=part,
                              values=(kv_slot1[:, :], dram["dil_v"][bass.ds(2 * i + part, 1)].rearrange("a p n -> p (a n)")),
                              turned_v=lambda: values_in(vnat1, vnew1, "att1", i, part))
            out_and_memory(1, mix1)
            cross(1)
            ffn(1)
            for t, (a, b) in enumerate(TILES):
                for half in range(2):
                    act.wait_ge(sem["answered"], at("answered", "norm_final", 0, 2 * t + half + 1))
                    c = slice(4 * half, 4 * half + 4)
                    act.dma_start(dram["y"][:, c, a:b], answer[:, c, a:b]).then_inc(stored["y"], 16)
            act.wait_ge(stored["k"], KV_STORES)
            act.wait_ge(stored["v"], KV_STORES)
            act.wait_ge(stored["u"], 16 * (PAIRS + 5))
            act.wait_ge(stored["y"], 16 * 6)

        @block.vector
        def _(dve):
            steps = [0]

            def past_waits():
                dve.sem_inc(gate_sem["dve"], 1)

            def zero(name):
                dve.memset(ones[:], 1.0)
                dve.memset(rs[:], 0.0).then_inc(sem["zeroed"], 1)
                dve.wait_ge(sem["zeroed"], at("zeroed", name, 0, 1))

            def add_square(source, turn, k, a, b, sq=None, order=None, chain=3):
                o = k if order is None else order
                if not isinstance(turn, int) or o >= chain:
                    dve.wait_ge(sem["added"], at("added", source, turn, o - chain + 1))
                dve.wait_ge(sem["squared"], at("squared", source, turn, k + 1))
                past_waits()
                dve.tensor_tensor(rs[:, a:b], sq_banks[k % 2][:, 0:b - a] if sq is None else sq, rs[:, a:b], ALU.add
                                  ).then_inc(sem["added"], 1)

            def low_part(source, turn, k, n, a, b):
                g, hi, lo = INTO[source]
                dve.wait_ge(sem["hi_ready"], at("hi_ready", source, turn, k + 1))
                past_waits()
                dve.scalar_tensor_tensor(flat(lo[:, n, a:b]), flat(x[:, n, a:b]), gains[:, g, n],
                                         flat(hi[:, n, a:b]).bitcast(F32), ALU.mult, ALU.subtract).then_inc(sem["lo_ready"], 1)

            def inverse(name):
                for t, (a, b) in enumerate(TILES):
                    dve.wait_ge(sem["rooted"], at("rooted", name, 0, t + 1))
                    dve.reciprocal(rs[:, a:b], rs[:, a:b]).then_inc(sem["rsqrted"], 1)
                dve.wait_ge(sem["rsqrted"], at("rsqrted", name, 0, 3))

            def split(phase, mix, hi, lo):
                for t, (a, b) in enumerate(TILES):
                    for q in range(4):
                        c = slice(2 * q, 2 * q + 2)
                        dve.wait_ge(sem["hi_ready"], at("hi_ready", phase, 0, 4 * t + q + 1))
                        dve.tensor_tensor(lo[:, c, a:b], mix[:, c, a:b], hi[:, c, a:b].bitcast(F32), ALU.subtract
                                          ).then_inc(sem["lo_ready"], 1)

            def empty(phase, turn, p, out, factor, w=TILE):
                dve.wait_ge(sem["tile_done"], at("tile_done", phase, turn, p + 1))
                dve.tensor_tensor(out, lin[tile_plan(phase)[p][0]][:, 0:w], factor, ALU.mult).then_inc(sem["freed_dve"], 1)

            def linear_out(phase):
                with dve.Fori(0, 4) as i:
                    for u in range(2):
                        for t, (a, b) in enumerate(TILES):
                            p = 3 * u + t
                            dve.wait_ge(sem["tile_done"], at("tile_done", phase, i, p + 1))
                            n = bass.ds(2 * i + u, 1)
                            xs = flat(x[:, n, a:b])
                            dve.tensor_tensor(xs, lin[tile_plan(phase)[p][0]][:, 0:TILE], xs, ALU.add
                                              ).then_inc(sem["freed_dve"], 1)
                            add_square(phase, i, p, a, b)
                            low_part(phase, i, p, n, a, b)

            def attention(phase, turn, kind, p, ps, mask, smask, part=0):
                n = len(JOBS[kind])
                before = part * (n + 1)
                scale = 1.0 / 16.0 if kind == "mem" else 1.0 / 8.0
                rows = 8 if kind == "mem" else 16

                def width(job):
                    return ps.shape[1] if job == "sample" else P * key_blocks(kind, job)[1]

                def place_of(job, u):
                    if job == "sample":
                        return ps[:, :]
                    return p[:, job % RING[kind], STRIDE[kind] * u:STRIDE[kind] * u + width(job)]

                def bias_of(job):
                    s, o = before + order_s(kind, job), order_s(kind, job) % 2
                    m = rows if job == "sample" else P
                    heads = (0,) if job == "sample" else JOBS[kind][job][1]
                    dve.wait_ge(sem["scored"], at("scored", phase, turn, s + 1))
                    sc = score_banks[o]
                    if kind == "mem":
                        dve.tensor_reduce(peak[0:m, 2 * o:2 * o + 1], sc[0:m, 0:MEM], AX_X, ALU.max).then_inc(sem["peaked"], 1)
                    else:
                        dve.wait_ge(sem["turned"], at("turned", phase, turn, before + (0 if job == "sample" else max(0, job - RING[kind] + 1))))
                        past_waits()
                        w = width(job)
                        for u, h in enumerate(heads):
                            c = 2 * o + u
                            msk = smask[:, :] if job == "sample" else mask[:, mask.shape[1] - w:]
                            start = NEG
                            if kind == "swa":
                                sc_ = 2 if job == "sample" else h
                                start = sink8[0:m, sc_:sc_ + 1]
                            at_ = 512 * u
                            op = dve.tensor_tensor_reduce(place_of(job, u), sc[0:m, at_:at_ + w], msk, 1.0, start,
                                                          ALU.add, ALU.max, peak[0:m, c:c + 1])
                        op.then_inc(sem["peaked"], 1)
                    dve.wait_ge(sem["peaked"], at("peaked", phase, turn, s + 1))
                    c = slice(2 * o, 2 * o + len(heads))
                    dve.tensor_scalar(bias[0:m, c], peak[0:m, c], -scale, None, ALU.mult).then_inc(sem["biased"], 1)

                def normalise(job):
                    s, o = before + order_s(kind, job), order_s(kind, job) % 2
                    m = rows if job == "sample" else P
                    heads = (0,) if job == "sample" else JOBS[kind][job][1]
                    c = slice(2 * o, 2 * o + len(heads))
                    dve.wait_ge(sem["exped"], at("exped", phase, turn, s + 1))
                    total = den
                    if kind == "swa":
                        dve.tensor_tensor(peak[0:m, c], den[0:m, c], sink_exp[0:m, c], ALU.add).then_inc(dve_step, 1)
                        dve.wait_ge(dve_step, turn * DVE_PER_TURN + (DVE_BASE + CONV_STEPS + s + 1))
                        total = peak
                    dve.reciprocal(inv[0:m, c], total[0:m, c]).then_inc(sem["inverted"], 1)
                    dve.wait_ge(sem["inverted"], at("inverted", phase, turn, s + 1))
                    if job == "sample" and kind != "mem":
                        w = ps.shape[1]
                        dve.tensor_scalar(sel[kind][:], token_mask[:], ps[:, w - 1:w], inv[0:m, c], ALU.mult, ALU.mult)
                        op = dve.tensor_scalar(ps[:, 0:w - 1], ps[:, 0:w - 1], inv[0:m, c], None, ALU.mult)
                    else:
                        for u in range(len(heads)):
                            dst = place_of(job, u)
                            op = dve.tensor_scalar(dst, dst, inv[0:m, 2 * o + u:2 * o + u + 1], None, ALU.mult)
                    op.then_inc(sem["normed"], 1)

                jobs = scoring(kind)
                bias_of(jobs[0])
                for last, job in zip(jobs, jobs[1:]):
                    bias_of(job)
                    normalise(last)
                normalise(jobs[-1])

            def spread(q, qd, ph, turn, part, at_freed):
                dve.wait_ge(sem["freed_dve"], at_freed)
                past_waits()
                cols = qd[:, :, :].rearrange("p b n -> p (b n)")
                dve.tensor_copy(cols[0:HEAD, 0:P:18], q[0:HEAD, SEQ:TOK])
                dve.tensor_copy(cols[HEAD:P, 1:P:18], q[HEAD:P, SEQ:TOK]).then_inc(sem["q_spread"], 1)

            def cross(l):
                ph = f"cross{l}"
                dve.wait_ge(sem["tile_done"], at("tile_done", ph, 0, 1))
                dve.memset(qdc[:], 0.0).then_inc(dve_step, 1)
                dve.wait_ge(dve_step, CROSS_STEP[l])
                with dve.Fori(0, CA_HEADS) as i:
                    dve.wait_ge(stored["k"], stored_before(l, 1, i))
                    empty(ph, i, 0, kc[:, 0, :], mem_rs[:], MEM)
                    for t, (a, b) in enumerate(TILES):
                        empty(ph, i, 1 + t, qc[:, 0, a:b], rs[:, a:b])
                    empty(ph, i, 4, kc[:, 1, :], mem_rs[:], MEM)
                    dve.wait_ge(stored["v"], stored_before(l, 1, i))
                    empty(ph, i, 5, vc[:, 0, :], mem_rs[:], MEM)
                    for t, (a, b) in enumerate(TILES):
                        empty(ph, i, 6 + t, qc[:, 1, a:b], rs[:, a:b])
                    dve.wait_ge(sem["freed_dve"], at("freed_dve", ph, i, 9))
                    past_waits()
                    for c in range(2):
                        op = dve.tensor_copy(qdc[:, c, :, :].rearrange("p b n -> p (b n)")[:, 0:64:9], qc[:, c, SEQ:TOK])
                    op.then_inc(sem["q_spread"], 1)
                    empty(ph, i, 9, vc[:, 1, :], mem_rs[:], MEM)
                    attention(ph, i, "mem", p_c, psc, None, None)
                zero(f"norm_ffn{l}")
                split(f"casplit{l}", mixc, g_hi, g_lo)
                linear_out(f"caout{l}")
                inverse(f"norm_ffn{l}")

            def ffn(l):
                ph = f"ffn{l}"
                def step(i):
                    for c in range(2):
                        for t, (a, b) in enumerate(TILES):
                            empty(ph, i, 6 * c + t, gate[:, a:b], rs[:, a:b])
                        for t, (a, b) in enumerate(TILES):
                            empty(ph, i, 6 * c + 3 + t, hid[:, a:b], rs[:, a:b])
                            dve.wait_ge(sem["gated"], at("gated", ph, i, 3 * c + t + 1))
                            dve.wait_ge(sem["freed_dve"], at("freed_dve", ph, i, 6 * c + 3 + t + 1))
                            dve.tensor_tensor(hid[:, a:b], hid[:, a:b], gate[:, a:b], ALU.mult).then_inc(sem["hid_done"], 1)
                            dve.wait_ge(sem["hid_hi"], at("hid_hi", ph, i, 3 * c + t + 1))
                            dve.tensor_tensor(hid_lo[:, c, a:b], hid[:, a:b], hid_hi[:, c, a:b].bitcast(F32), ALU.subtract
                                              ).then_inc(sem["hid_lo"], 1)

                def add(i, half, t, n):
                    a, b = TILES[t]
                    p = 12 + 12 * half + 4 * t + n
                    dve.wait_ge(sem["tile_done"], at("tile_done", ph, i, p + 1))
                    dve.tensor_tensor(x[:, 4 * half + n, a:b], lin[tile_plan(ph)[p][0]][:, 0:TILE],
                                      x[:, 4 * half + n, a:b], ALU.add).then_inc(sem["freed_dve"], 1)

                order = [(half, t, n) for half in range(2) for t in range(3) for n in range(4)]
                with dve.Fori(0, FFN_STEPS - 1) as i:
                    step(i)
                    for half, t, n in order:
                        add(i, half, t, n)
                step(FFN_STEPS - 1)
                source, name = (("into_mix1", "norm_mix1"), ("into_final", "norm_final"))[l]
                zero(name)

                def squares(k, o, chain):
                    half, t, n = order[k]
                    a, b = TILES[t]
                    add_square(source, 0, k, a, b, sq=sq_all[:, 4 * half + n, a:b], order=o, chain=chain)

                def low(k):
                    half, t, n = order[k]
                    low_part(source, 0, k, slice(4 * half + n, 4 * half + n + 1), *TILES[t])

                for k, (half, t, n) in enumerate(order):
                    add(FFN_STEPS - 1, half, t, n)
                    if l == 0 and k >= 4:
                        low(k - 4)
                    if l == 1 and k:
                        squares(k - 1, k - 1, 1)
                if l == 1:
                    squares(23, 23, 1)
                else:
                    for t in range(3):
                        for j, k in enumerate(k for k in range(24) if order[k][1] == t):
                            squares(k, CH * t + j, 1)
                        if t == 0:
                            for k in range(20, 24):
                                low(k)
                inverse(name)

            zero("norm_mix0")
            dve.wait_ge(loads["consts"], 48)
            for t, (a, b) in enumerate(TILES):
                for n in range(CH):
                    if t == 0 and n % 4 == 0:
                        dve.wait_ge(loads[f"x0{n // 4}"], 16)
                    elif n == 0:
                        dve.wait_ge(loads[f"x{t}"], 16)
                    add_square("into_mix0", 0, CH * t + n, a, b, chain=1)
                    low_part("into_mix0", 0, CH * t + n, slice(n, n + 1), a, b)
            inverse("norm_mix0")
            for j, dst in enumerate((k0, v0)):
                for t, (a, b) in enumerate(TILES):
                    empty("kv0", 0, 3 * j + t, dst[:, a:b], rs[:, a:b])
            dve.wait_ge(loads["att0"], ATT0_LOADS)
            dve.tensor_tensor(rs2[:], rs[:], rs[:], ALU.mult)
            dve.memset(conv_u[:, 0:2], 0.0)
            dve.memset(qd0[:], 0.0).then_inc(dve_step, 1)
            dve.wait_ge(dve_step, 1)
            with dve.Fori(0, PAIRS) as i:
                def step(k):
                    dve.wait_ge(dve_step, i * DVE_PER_TURN + (DVE_BASE + k))

                dve.tensor_copy(cur[:], stash[:, bass.ds(i, 1), :].rearrange("p a n -> p (a n)")).then_inc(dve_step, 1)
                step(1)
                dve.tensor_scalar(sink8[:], cur[:, 19:22], 8.0, None, ALU.mult).then_inc(dve_step, 1)
                step(2)
                for t, (a, b) in enumerate(TILES):
                    empty("att0", i, t, q0[:, a:b], rs[:, a:b])
                spread(q0, qd0, "att0", i, 0, at("freed_dve", "att0", i, 3))
                for t, (a, b) in enumerate(TILES):
                    empty("att0", i, 3 + t, cgate[:, a:b], rs2[:, a:b])
                dve.wait_ge(stored["u"], 16 * i + 16)
                for t, (a, b) in enumerate(TILES):
                    dve.wait_ge(sem["freed_dve"], at("freed_dve", "att0", i, 3 + t + 1))
                    empty("att0", i, 6 + t, conv_u[:, 2 + a:2 + b], cgate[:, a:b])
                dve.wait_ge(sem["freed_dve"], at("freed_dve", "att0", i, 9))
                past = lambda r: cur[:, 3 + 8 * r:11 + 8 * r]
                dve.tensor_scalar(conv_t[:, 0:SEQ], conv_u[:, 0:SEQ], cur[:, 0:1], None, ALU.mult)
                dve.tensor_scalar(conv_t[:, SEQ:TOK], past(0), cur[:, 0:1], None, ALU.mult).then_inc(dve_step, 1)
                step(3)
                dve.scalar_tensor_tensor(conv_t[:, 0:SEQ], conv_u[:, 1:SEQ + 1], cur[:, 1:2], conv_t[:, 0:SEQ], ALU.mult, ALU.add)
                dve.scalar_tensor_tensor(conv_t[:, SEQ:TOK], past(1), cur[:, 1:2], conv_t[:, SEQ:TOK], ALU.mult, ALU.add
                                         ).then_inc(dve_step, 1)
                step(4)
                dve.scalar_tensor_tensor(conv_t[:, :], conv_u[:, 2:2 + TOK], cur[:, 2:3], conv_t[:, :], ALU.mult, ALU.add
                                         ).then_inc(dve_step, 1)
                step(5)
                dve.tensor_tensor(conv_t[:, :], conv_t[:, :], rs[:, :], ALU.mult).then_inc(dve_step, 1)
                step(6)
                for t, (a, b) in enumerate(TILES):
                    empty("att0", i, 9 + t, flat(mix0[:, bass.ds(i, 1), a:b]), conv_t[:, a:b])
                attention("att0", i, "swa", p0, ps0, mask0, smask0)

            def out_and_memory(l, mix):
                ph = f"norm_ca{l}"
                zero(ph)
                split(f"split{l}", mix, h_hi, h_lo)
                g = GAINS.index(f"mem{l}")
                for half, dst in enumerate((mem_sum[:], mem_half[:])):
                    dve.wait_ge(sem["mem_squared"], at("mem_squared", ph, 0, half + 1))
                    dve.tensor_reduce(dst, ps_s[:, :].rearrange("p (c n) -> p n c", c=4), AX_X, ALU.add
                                      ).then_inc(sem["mem_added"], 1)
                    dve.wait_ge(sem["mem_hi"], at("mem_hi", ph, 0, half + 1))
                    for c in range(4 * half, 4 * half + 4):
                        op = dve.scalar_tensor_tensor(mem_lo[:, c, :], mem_raw[:, c, :], gains[:, g, c:c + 1],
                                                      mem_hi[:, c, :].bitcast(F32), ALU.mult, ALU.subtract)
                    op.then_inc(sem["mem_lo"], 1)
                dve.wait_ge(sem["mem_added"], at("mem_added", ph, 0, 2))
                dve.tensor_tensor(mem_sum[:], mem_sum[:], mem_half[:], ALU.add).then_inc(sem["mem_added"], 1)
                linear_out(f"out{l}")
                inverse(ph)
                dve.wait_ge(sem["mem_rooted"], at("mem_rooted", ph, 0, 1))
                dve.reciprocal(mem_rs[:], mem_rs[:]).then_inc(sem["mem_rsqrted"], 1)
                dve.wait_ge(sem["mem_rsqrted"], at("mem_rsqrted", ph, 0, 1))

            out_and_memory(0, mix0)
            cross(0)
            ffn(0)
            dve.wait_ge(loads["pool1"], 64)
            steps[0] = POOL_STEP

            def chained(op):
                steps[0] += 1
                op.then_inc(dve_step, 1)
                dve.wait_ge(dve_step, steps[0])

            chained(dve.memset(pool_u[:, 0:POOL_PAD], 0.0))
            for g, w in enumerate(POOL_WINDOWS):
                if g:
                    dve.wait_ge(sem["delta_ready"], at("delta_ready", "pool1", 0, g))
                    dve.wait_ge(stored["u"], 16 * (PAIRS + g + 1))
                for t, (a, b) in enumerate(TILES):
                    empty("pool1", 0, 3 * g + t, pool_u[:, POOL_PAD + a:POOL_PAD + b], rs[:, a:b])
                dve.wait_ge(sem["freed_dve"], at("freed_dve", "pool1", 0, 3 * g + 3))
                if g >= 2:
                    dve.wait_ge(sem["pooled"], at("pooled", "pool1", 0, 3 * (g - 1)))
                src, n, have = pool_u, POOL_PAD + SEQ, 1
                for dst in (pool_a, pool_b, pool_a, pool_b)[:g + 1]:
                    n -= have
                    chained(dve.tensor_tensor(dst[:, 0:n], src[:, have:have + n], src[:, 0:n], ALU.add))
                    src, have = dst, 2 * have
                win = src[:, 16 - w:16 - w + SEQ]
                d = pool_d[:, g % 2, :]
                u = pool_u[:, POOL_PAD:]
                head = pool_s[:, :, :].rearrange("p a b -> p (a b)")
                dve.scalar_tensor_tensor(d[:, 16:SEQ], win[:, 16:SEQ], 1.0 / w, u[:, 16:SEQ], ALU.mult, ALU.subtract)
                chained(dve.tensor_tensor(head, win[:, 0:16], pool_rcp[:, g, :], ALU.mult))
                chained(dve.tensor_tensor(d[:, 0:16], head, u[:, 0:16], ALU.subtract))
                chained(dve.tensor_reduce(pool_s[:, 0, :], pool_hist[:, g, :, 16 - w:15], AX_X, ALU.add))
                chained(dve.tensor_tensor(pool_s[:, 1, :], pool_s[:, 0, :], u[:, SEQ:TOK], ALU.add))
                dve.scalar_tensor_tensor(d[:, SEQ:TOK], pool_s[:, 1, :], 1.0 / w, u[:, SEQ:TOK], ALU.mult, ALU.subtract
                                         ).then_inc(sem["delta_ready"], 1)
            dve.wait_ge(sem["pooled_out"], at("pooled_out", "pool1", 0, 12))
            dve.wait_ge(sem["delta_ready"], at("delta_ready", "pool1", 0, 4))
            chained(dve.memset(qd1[:], 0.0))
            assert steps[0] == ATT1_STEP
            dve.wait_ge(loads["att1"], 32)
            with dve.Fori(0, PAIRS // 2) as i:
                for part in range(2):
                    for t, (a, b) in enumerate(TILES):
                        empty("att1", i, 9 * part + t, q1[:, a:b], rs[:, a:b])
                    spread(q1, qd1, "att1", i, part, at("freed_dve", "att1", i, 9 * part + 3))
                    for j, (dst, name) in enumerate(((k1, "k"), (v1, "v"))):
                        dve.wait_ge(stored[name], stored_before(1, 0, i, part))
                        for t, (a, b) in enumerate(TILES):
                            empty("att1", i, 9 * part + 3 * j + 3 + t, dst[:, a:b], rs[:, a:b])
                    attention("att1", i, "dil", p1, ps1, mask1, smask1, part=part)
            out_and_memory(1, mix1)
            cross(1)
            ffn(1)
            g = INTO["into_final"][0]
            for t, (a, b) in enumerate(TILES):
                for c in range(CH):
                    op = dve.scalar_tensor_tensor(answer[:, c, a:b], x[:, c, a:b], gains[:, g, c:c + 1], rs[:, a:b],
                                                  ALU.mult, ALU.mult)
                    if c % 4 == 3:
                        op.then_inc(sem["answered"], 1)



def unit_list(i):
    def into(w, cols):
        return np.ascontiguousarray(w[:, cols].reshape(CH, P, P).transpose(1, 0, 2).reshape(P, D))

    def block(w, n):
        return into(w, slice(P * n, P * n + P))

    units = []
    pair_cols = [np.r_[HEAD * c:HEAD * c + HEAD, HEAD * (4 + c):HEAD * (4 + c) + HEAD] for c in range(PAIRS)]
    for l in range(2):
        if l == 0:
            w = i["w_in_even"][0]
            b0, c0, x0, q0, k0, v0 = 0, 512, 1024, 1536, 2048, 2176
            units += [block(w[:, k0:], 0), block(w[:, v0:], 0)]
            for c in range(PAIRS):
                units += [into(w, q0 + pair_cols[c]), block(w[:, c0:], c), block(w[:, x0:], c), block(w[:, b0:], c)]
            wo = i["w_out_even"][0]
            wo = np.concatenate([wo[:512]] + [wo[512 + pair_cols[c]] for c in range(PAIRS)])
        else:
            w = i["w_in_odd"][0]
            units += [block(w, g) for g in range(4)]
            for c in range(PAIRS):
                units += [block(w[:, o:], c) for o in (512, 1024, 1536)]
            wo = i["w_out_odd"][0]
        units += [block(wo, n) for n in range(CH)]
        wkv, wq = i["w_ca_kv"][l], i["w_ca_q"][l]
        for h in range(CA_HEADS):
            wk, wv = wkv[:, :D], wkv[:, D:]
            units += [block(w, 2 * h + c) for w, c in ((wk, 0), (wq, 0), (wk, 1), (wv, 0), (wq, 1), (wv, 1))]
        units += [block(i["w_ca_o"][l], n) for n in range(CH)]
        wi, wo = i["w_ffn_in"][l], i["w_ffn_out"][l]
        for s in range(FFN_STEPS):
            for n in (2 * s, 2 * s + 1):
                units += [block(wi, n), block(wi[:, FFN:], n)]
            rows = wo[256 * s:256 * s + 256].reshape(2, P, 2, 512)
            for half in range(2):
                units.append(np.ascontiguousarray(rows[:, :, half].transpose(1, 0, 2).reshape(P, D)))
    return np.stack(units)


def masks():
    def table(f, width):
        delta = (width - P) + np.arange(P)[:, None] - np.arange(width)[None, :]
        return f(delta).astype(np.float32)

    def window(delta):
        return np.where((delta >= 0) & (delta <= P), 0.0, NEG)

    def dilated(delta):
        n = sum(((delta >= 0) & (delta <= w) & (delta % d == 0)).astype(int) for w, d in DILATIONS)
        return np.where(n > 0, 8.0 * np.log(np.maximum(n, 1)), NEG)

    new = np.zeros((16, 385), np.float32)
    new[:, 384] = 8.0 * np.log(3.0)
    return table(window, 256), table(dilated, 1024), np.zeros((16, 129), np.float32), new


def host_inputs(i):
    fm = lambda a: np.ascontiguousarray(a)
    out = {"w": unit_list(i)}
    xs = np.concatenate([i["x_prompt"][0], i["x_sample"][:, 0]])
    out["x"] = fm(xs.T.reshape(CH, P, TOK).transpose(1, 0, 2))
    out["mem"] = fm(i["mem_prompt"][0].T.reshape(CH, P, MEM).transpose(1, 0, 2))
    g = np.stack([i["norm_mix"][0], i["norm_mix"][1], i["norm_ca"][0], i["norm_ca"][1], i["norm_mem"][0],
                  i["norm_mem"][1], i["norm_ffn"][0], i["norm_ffn"][1], i["norm_final"]])
    out["gains"] = fm(g.reshape(len(GAINS), CH, P).transpose(2, 0, 1))
    out["ident"] = np.eye(P, dtype=np.float32)
    out["token_mask"] = fm(np.repeat(np.eye(BATCH_S, dtype=np.float32), 2, axis=0))
    out["cache_conv"] = fm(i["cache_conv"][0])
    out["state_pool"] = fm(i["state_pool"][0])
    out["swa_k"] = fm(i["cache_swa_k"][0].transpose(2, 3, 0, 1).reshape(P, BATCH_S, P))
    out["swa_v"] = fm(i["cache_swa_v"][0].transpose(1, 0, 2, 3).reshape(P, BATCH_S, 1, P))
    stash = np.zeros((P, PAIRS, STASH), np.float32)
    stash[:, :, 0:3] = i["conv_w"][0].reshape(CONV_W, PAIRS, P).transpose(2, 1, 0)
    stash[:, :, 3:19] = i["cache_conv"][0].reshape(BATCH_S, 2, PAIRS, P).transpose(3, 2, 1, 0).reshape(P, PAIRS, 16)
    sinks = i["sinks"][0].reshape(2, PAIRS)
    stash[:, :, 19:21] = sinks.T[None]
    stash[0:16, :, 21] = sinks[np.arange(16) % 2]
    out["stash"] = stash
    out["mask0"], out["mask1"], out["smask0"], out["smask1"] = masks()
    out["pool_hist"] = fm(i["state_pool"][0].reshape(BATCH_S, POOL_PAD, 4, P).transpose(3, 2, 0, 1))
    out["pool_w"] = fm(i["pool_w"][0].transpose(1, 0, 2))
    rcp = 1.0 / np.minimum(np.arange(16)[None, :] + 1, np.array(POOL_WINDOWS)[:, None])
    out["pool_rcp"] = fm(np.broadcast_to(rcp.astype(np.float32), (P, 4, 16)))
    out["pool_gain"] = fm(i["pool_scale"][0].reshape(4, P).T)
    rows = np.concatenate([2048 - w + d * np.arange(P) for w, d in DILATIONS])
    dk = i["cache_dil_k"][0][:, rows].reshape(BATCH_S, 384, PAIRS, P)
    dv = i["cache_dil_v"][0][:, rows].reshape(BATCH_S, 3, P, PAIRS, P)
    out["dil_k"] = fm(dk.transpose(2, 3, 0, 1).reshape(PAIRS, P, -1))
    out["dil_v"] = fm(dv.transpose(3, 2, 0, 1, 4).reshape(PAIRS, P, -1))
    mk = i["cache_mem_k"].reshape(2, BATCH_S, MEM, CA_HEADS, 2, P)
    out["mem_cache_k"] = fm(mk.transpose(0, 3, 5, 1, 4, 2).reshape(2, CA_HEADS, P, -1))
    mv = i["cache_mem_v"].reshape(2, BATCH_S, 2, P, CA_HEADS, 2 * P)
    out["mem_cache_v"] = fm(mv.transpose(0, 4, 3, 1, 2, 5).reshape(2, CA_HEADS, P, -1))
    return out


OUTS = {"y": (P, CH, TOK), "conv_past": (BATCH_S, 512), "pool_past": (BATCH_S, 14, 512), "swa_k_out": (P, P + BATCH_S),
        "swa_v_out": (P, P + BATCH_S), "conv_out": (PAIRS, P, 10), "pool_out": (4, P, 23), "dil_k_out": (PAIRS, P, TOK),
        "dil_v_out": (PAIRS, P, TOK), "mem_k": (2, CA_HEADS, P, 2, MEM), "mem_v": (2, CA_HEADS, P, 2, MEM)}


def kernel(**inputs):
    import concourse.bacc as bacc
    from concourse.bass_utils import run_bass_kernel_spmd

    arrays = host_inputs({k: np.asarray(v) for k, v in inputs.items()})
    nc = bacc.Bacc("TRN2", target_bir_lowering=False, num_devices=1)
    dram = {n: nc.dram_tensor(f"in_{n}", a.shape, F32, kind="ExternalInput").ap() for n, a in arrays.items()}
    dram |= {n: nc.dram_tensor(f"out_{n}", s, F32, kind="ExternalOutput").ap() for n, s in OUTS.items()}
    program(nc, dram)
    r = run_bass_kernel_spmd(nc, [{f"in_{n}": a for n, a in arrays.items()}], core_ids=[0]).results[0]
    o = {n: np.asarray(r[f"out_{n}"]) for n in OUTS}

    y = o["y"].transpose(2, 1, 0).reshape(TOK, D)
    conv = o["conv_out"].transpose(2, 0, 1).reshape(10, 512)
    pooled = o["pool_out"].transpose(2, 0, 1).reshape(23, 512)
    swa = {n: o[f"swa_{n}_out"].T.reshape(P + BATCH_S, 2, HEAD) for n in "kv"}
    dil = {n: o[f"dil_{n}_out"].transpose(2, 0, 1).reshape(TOK, 8, HEAD) for n in "kv"}
    mem = {n: o[f"mem_{n}"].transpose(0, 4, 1, 3, 2).reshape(2, 1, MEM, CA_HEADS, 2 * P) for n in "kv"}
    conv_s = np.stack([o["conv_past"], conv[2:]], axis=1)
    pool_s = np.concatenate([o["pool_past"], pooled[15:, None]], axis=1)
    return (y[None, :SEQ], y[SEQ:, None],
            conv[None, None, :2], swa["k"][None, None, :P], swa["v"][None, None, :P],
            pooled[None, None, :15], dil["k"][None, None, :SEQ], dil["v"][None, None, :SEQ],
            mem["k"], mem["v"],
            conv_s[None], swa["k"][P:][None, :, None], swa["v"][P:][None, :, None],
            pool_s[None], dil["k"][SEQ:][None, :, None], dil["v"][SEQ:][None, :, None])
```
